# Optimizing a Trainium2 kernel written in Bass

```python
import jax, jax.numpy as jnp
from jax import lax
import numpy as np

D_MODEL = 1024
BATCH = 1
SEQ = 128
DEPTH = 2
DEC_BATCH = 1
DEC_SEQ = 512
PAST_LEN = 128

GRID_W = 64
EPS = 1e-6
ROPE_THETA = 10000.0
QBLOCK = 128
NEG_INF = -1e30

NA_HEADS = 6
NA_DH = 64
NA_WIN_R = 8
NA_WIN_C = 16
NA_QB = NA_WIN_C
NA_KB = 2 * NA_WIN_C
NA_WIDTH = NA_HEADS * NA_DH

POOL_WINDOWS = (2, 4, 8, 16)
POOL_G = 64
POOL_WIDTH = POOL_G * len(POOL_WINDOWS)

MLA_HEADS = 6
MLA_NOPE = 64
MLA_ROPE = 32
MLA_QK = MLA_NOPE + MLA_ROPE
MLA_V = 64
MLA_Q_RANK = 256
MLA_KV_RANK = 128
MLA_WIDTH = MLA_HEADS * MLA_V

MIX_WIDTH = NA_WIDTH + POOL_WIDTH + MLA_WIDTH
IN_SPLITS = (NA_WIDTH, NA_WIDTH, NA_WIDTH, POOL_WIDTH, MLA_Q_RANK, MLA_KV_RANK, MLA_ROPE)
IN_WIDTH = sum(IN_SPLITS)

PEER_HEADS = 8
PEER_NKEYS = 128
PEER_NEXP = PEER_NKEYS * PEER_NKEYS
PEER_DKEY = 128
PEER_TOPK = 16
PEER_TOK_BLOCK = 128

kernel_name = 'hybrid_flow_backbone_step'

def rms_norm(x, g):
    xf = x.astype(jnp.float32)
    y = xf * lax.rsqrt(jnp.mean(xf * xf, axis=-1, keepdims=True) + EPS)
    return (y * g.astype(jnp.float32)).astype(x.dtype)

def modulation(cond, w_mod, b_mod):
    m = jax.nn.silu(cond) @ w_mod + b_mod
    return jnp.split(m[:, None, :], 6, axis=-1)

def modulate(x, shift, scale):
    return x * (1 + scale) + shift

def axial_rope(x):
    T = x.shape[1]
    t = jnp.arange(T)
    half = MLA_ROPE // 2
    inv = ROPE_THETA ** (-jnp.arange(0, half, 2, dtype=jnp.float32) / half)
    xf = x.astype(jnp.float32)

    def rot(xa, pos):
        ang = pos.astype(jnp.float32)[:, None] * inv[None, :]
        cos = jnp.cos(ang)[None, :, None, :]
        sin = jnp.sin(ang)[None, :, None, :]
        x1, x2 = jnp.split(xa, 2, axis=-1)
        return jnp.concatenate([x1 * cos - x2 * sin, x1 * sin + x2 * cos], axis=-1)

    out = jnp.concatenate([rot(xf[..., :half], t // GRID_W), rot(xf[..., half:], t % GRID_W)], axis=-1)
    return out.astype(x.dtype)

def rope_tail(x):
    return jnp.concatenate([x[..., :MLA_NOPE], axial_rope(x[..., MLA_NOPE:])], axis=-1)

def dense_block_attn(q, k, v, scale):
    B, T, H, dq = q.shape
    dv = v.shape[-1]
    nb = T // QBLOCK
    qb = jnp.moveaxis(q.reshape(B, nb, QBLOCK, H, dq), 1, 0)

    def one_block(qi):
        s = jnp.einsum('bqhd,bshd->bhqs', qi, k, preferred_element_type=jnp.float32) * scale
        p = jax.nn.softmax(s, axis=-1)
        return jnp.einsum('bhqs,bshd->bqhd', p.astype(v.dtype), v)

    o = lax.map(one_block, qb)
    return jnp.moveaxis(o, 0, 1).reshape(B, T, H * dv)

def nat_latent_attn(q, k, v, kc, vc, rel_bias):
    B, T, H, dh = q.shape
    rows = T // GRID_W
    wr = min(NA_WIN_R, rows)
    ncb = GRID_W // NA_QB
    scale = dh ** -0.5
    qcol = np.arange(GRID_W).reshape(ncb, NA_QB)
    cstart = np.clip(qcol - NA_WIN_C // 2, 0, GRID_W - NA_WIN_C)
    kb = np.clip(np.arange(ncb) * NA_QB - NA_WIN_C // 2, 0, GRID_W - NA_KB)
    kcol = kb[:, None] + np.arange(NA_KB)
    col_ok = (kcol[:, None, :] >= cstart[..., None]) & (kcol[:, None, :] < cstart[..., None] + NA_WIN_C)
    dc_idx = np.clip(kcol[:, None, :] - qcol[..., None] + NA_WIN_C - 1, 0, 2 * NA_WIN_C - 2)
    kg = k.reshape(B, rows, GRID_W, H, dh)
    vg = v.reshape(B, rows, GRID_W, H, dh)
    kcb = kg[:, :, kcol]
    vcb = vg[:, :, kcol]
    bias_c = rel_bias[:, :, dc_idx]
    qr = jnp.moveaxis(q.reshape(B, rows, ncb, NA_QB, H, dh), 1, 0)
    mask = jnp.asarray(col_ok)[None, None, :, :, None, :]

    def one_row(args):
        r, q_r = args
        rs = jnp.clip(r - NA_WIN_R // 2, 0, rows - wr)
        k_band = lax.dynamic_slice_in_dim(kcb, rs, wr, axis=1)
        v_band = lax.dynamic_slice_in_dim(vcb, rs, wr, axis=1)
        dr_idx = rs + jnp.arange(wr) - r + NA_WIN_R - 1
        bias = jnp.transpose(bias_c[:, dr_idx], (0, 2, 3, 1, 4))
        s_loc = jnp.einsum('bnqhd,bwnkhd->bhnqwk', q_r, k_band, preferred_element_type=jnp.float32) * scale
        s_loc = jnp.where(mask, s_loc + bias[None].astype(jnp.float32), NEG_INF)
        s_ctx = jnp.einsum('bnqhd,blhd->bhnql', q_r, kc, preferred_element_type=jnp.float32) * scale
        s = jnp.concatenate([s_loc.reshape(B, H, ncb, NA_QB, wr * NA_KB), s_ctx], axis=-1)
        p = jax.nn.softmax(s, axis=-1).astype(v.dtype)
        p_loc = p[..., :wr * NA_KB].reshape(B, H, ncb, NA_QB, wr, NA_KB)
        p_ctx = p[..., wr * NA_KB:]
        return (jnp.einsum('bhnqwk,bwnkhd->bnqhd', p_loc, v_band)
                + jnp.einsum('bhnql,blhd->bnqhd', p_ctx, vc))

    o = lax.map(one_row, (jnp.arange(rows), qr))
    return jnp.moveaxis(o, 0, 1).reshape(B, T, H * dh)

def pool_mixer(p, w_pool, pool_scale):
    B, L, _ = p.shape
    ng = len(POOL_WINDOWS)
    pf = p.astype(jnp.float32).reshape(B, L, ng, POOL_G)
    csum = jnp.concatenate([jnp.zeros((B, 1, ng, POOL_G), jnp.float32), jnp.cumsum(pf, axis=1)], axis=1)
    t = jnp.arange(L)
    diffs = []
    for gi, w in enumerate(POOL_WINDOWS):
        lo = jnp.clip(t - w // 2, 0, L)
        hi = jnp.clip(t + (w - w // 2), 0, L)
        cg = csum[:, :, gi]
        mean = (cg[:, hi] - cg[:, lo]) / (hi - lo).astype(jnp.float32)[None, :, None]
        diffs.append(mean - pf[:, :, gi])
    d = jnp.stack(diffs, axis=2).astype(p.dtype)
    y = jnp.einsum('blgc,gcd->blgd', d, w_pool).reshape(B, L, POOL_WIDTH)
    return y * pool_scale

def peer(h, wq, sub_keys, u, v):
    B, L, D = h.shape
    half = PEER_DKEY // 2
    xb_all = h.reshape(-1, PEER_TOK_BLOCK, D)

    def one_block(xb):
        n = xb.shape[0]
        q = (xb @ wq).reshape(n, PEER_HEADS, 2, half)
        s = jnp.einsum('nhpk,pmk->nhpm', q, sub_keys, preferred_element_type=jnp.float32)
        sv, si = lax.top_k(s, PEER_TOPK)
        cand_s = (sv[:, :, 0, :, None] + sv[:, :, 1, None, :]).reshape(n, PEER_HEADS, PEER_TOPK * PEER_TOPK)
        cand_i = (si[:, :, 0, :, None] * PEER_NKEYS + si[:, :, 1, None, :]).reshape(n, PEER_HEADS, PEER_TOPK * PEER_TOPK)
        top_s, top_j = lax.top_k(cand_s, PEER_TOPK)
        e = jnp.take_along_axis(cand_i, top_j, axis=-1)
        g = jax.nn.softmax(top_s, axis=-1)
        act = jax.nn.gelu(jnp.einsum('nd,nhkd->nhk', xb, u[e], preferred_element_type=jnp.float32))
        return jnp.einsum('nhk,nhkd->nd', (g * act).astype(v.dtype), v[e])

    y = lax.map(one_block, xb_all)
    return y.reshape(B, L, D)

def branch_inputs(h, lp):
    B, L, _ = h.shape
    z = h @ lp['w_in']
    idx = np.cumsum(IN_SPLITS)[:-1].tolist()
    q_na, k_na, v_na, p, cq, ckv, krope = jnp.split(z, idx, axis=-1)
    q_na = rms_norm(q_na.reshape(B, L, NA_HEADS, NA_DH), lp['na_q_norm'])
    k_na = rms_norm(k_na.reshape(B, L, NA_HEADS, NA_DH), lp['na_k_norm'])
    v_na = v_na.reshape(B, L, NA_HEADS, NA_DH)
    cq = rms_norm(cq, lp['mla_cq_norm'])
    q_mla = rms_norm(jnp.einsum('blr,rhe->blhe', cq, lp['mla_w_uq']), lp['mla_q_norm'])
    ckv = rms_norm(ckv, lp['mla_ckv_norm'])
    return q_na, k_na, v_na, p, q_mla, ckv, krope

def mla_kv(ckv, krope, w_ukv, k_norm):
    kv = jnp.einsum('blr,rhe->blhe', ckv, w_ukv)
    k_nope, v = kv[..., :MLA_NOPE], kv[..., MLA_NOPE:]
    k_rope = jnp.broadcast_to(krope[:, :, None, :], k_nope.shape[:-1] + (MLA_ROPE,))
    k = rms_norm(jnp.concatenate([k_nope, k_rope], axis=-1), k_norm)
    return k, v

def context_layer(x, c_ctx, lp):
    sh1, sc1, g1, sh2, sc2, g2 = modulation(c_ctx[None, :], lp['w_mod'], lp['b_mod'])
    h = modulate(rms_norm(x, lp['norm1']), sh1, sc1)
    q_na, k_na, v_na, p, q_mla, ckv, krope = branch_inputs(h, lp)
    o_na = dense_block_attn(q_na, k_na, v_na, NA_DH ** -0.5)
    o_pool = pool_mixer(p, lp['pool_w'], lp['pool_scale'])
    k_mla, v_mla = mla_kv(ckv, krope, lp['mla_w_ukv'], lp['mla_k_norm'])
    o_mla = dense_block_attn(q_mla, k_mla, v_mla, MLA_QK ** -0.5)
    x = x + g1 * (jnp.concatenate([o_na, o_pool, o_mla], axis=-1) @ lp['w_out'])
    h2 = modulate(rms_norm(x, lp['norm2']), sh2, sc2)
    x = x + g2 * peer(h2, lp['peer_wq'], lp['peer_subkeys'], lp['peer_u'], lp['peer_v'])
    return x, k_na, v_na, ckv, krope

def latent_layer(x, c, kc_na, vc_na, ckv_c, krope_c, lp):
    sh1, sc1, g1, sh2, sc2, g2 = modulation(c, lp['w_mod'], lp['b_mod'])
    h = modulate(rms_norm(x, lp['norm1']), sh1, sc1)
    q_na, k_na, v_na, p, q_mla, ckv, krope = branch_inputs(h, lp)
    o_na = nat_latent_attn(q_na, k_na, v_na, kc_na, vc_na, lp['na_rel_bias'])
    o_pool = pool_mixer(p, lp['pool_w'], lp['pool_scale'])
    k_lat, v_lat = mla_kv(ckv, krope, lp['mla_w_ukv'], lp['mla_k_norm'])
    k_ctx, v_ctx = mla_kv(ckv_c, krope_c, lp['mla_w_ukv'], lp['mla_k_norm'])
    q_mla = rope_tail(q_mla)
    k_lat = rope_tail(k_lat)
    o_mla = dense_block_attn(q_mla, jnp.concatenate([k_lat, k_ctx], axis=1),
                             jnp.concatenate([v_lat, v_ctx], axis=1), MLA_QK ** -0.5)
    x = x + g1 * (jnp.concatenate([o_na, o_pool, o_mla], axis=-1) @ lp['w_out'])
    h2 = modulate(rms_norm(x, lp['norm2']), sh2, sc2)
    x = x + g2 * peer(h2, lp['peer_wq'], lp['peer_subkeys'], lp['peer_u'], lp['peer_v'])
    return x

def setup_inputs(seed: int = 0) -> dict:
    key = jax.random.key(seed)
    keys = iter(jax.random.split(key, 32))

    def nrm(shape, std):
        return jax.random.normal(next(keys), shape, jnp.float32) * std

    def gain(shape):
        return 1.0 + nrm(shape, 0.05)

    D = D_MODEL
    return {
        'x_prompt': nrm((BATCH, SEQ, D), 1.0),
        'x_sample': nrm((DEC_BATCH, DEC_SEQ, D), 1.0),
        'c': nrm((DEC_BATCH, D), 1.0),
        'cache_nat_k': nrm((DEC_BATCH, DEPTH, PAST_LEN, NA_HEADS, NA_DH), 1.0),
        'cache_nat_v': nrm((DEC_BATCH, DEPTH, PAST_LEN, NA_HEADS, NA_DH), 1.0),
        'cache_mla_ckv': nrm((DEC_BATCH, DEPTH, PAST_LEN, MLA_KV_RANK), 1.0),
        'cache_mla_krope': nrm((DEC_BATCH, DEPTH, PAST_LEN, MLA_ROPE), 1.0),
        'c_ctx': nrm((D,), 1.0),
        'w_mod': nrm((DEPTH, D, 6 * D), 0.5 * D ** -0.5),
        'b_mod': nrm((DEPTH, 6 * D), 0.02),
        'norm1': gain((DEPTH, D)),
        'norm2': gain((DEPTH, D)),
        'w_in': nrm((DEPTH, D, IN_WIDTH), D ** -0.5),
        'na_q_norm': gain((DEPTH, NA_DH)),
        'na_k_norm': gain((DEPTH, NA_DH)),
        'na_rel_bias': nrm((DEPTH, NA_HEADS, 2 * NA_WIN_R - 1, 2 * NA_WIN_C - 1), 0.2),
        'pool_w': nrm((DEPTH, len(POOL_WINDOWS), POOL_G, POOL_G), POOL_G ** -0.5),
        'pool_scale': gain((DEPTH, POOL_WIDTH)),
        'mla_cq_norm': gain((DEPTH, MLA_Q_RANK)),
        'mla_ckv_norm': gain((DEPTH, MLA_KV_RANK)),
        'mla_w_uq': nrm((DEPTH, MLA_Q_RANK, MLA_HEADS, MLA_QK), MLA_Q_RANK ** -0.5),
        'mla_w_ukv': nrm((DEPTH, MLA_KV_RANK, MLA_HEADS, MLA_NOPE + MLA_V), MLA_KV_RANK ** -0.5),
        'mla_q_norm': gain((DEPTH, MLA_QK)),
        'mla_k_norm': gain((DEPTH, MLA_QK)),
        'w_out': nrm((DEPTH, MIX_WIDTH, D), MIX_WIDTH ** -0.5),
        'peer_wq': nrm((DEPTH, D, PEER_HEADS * PEER_DKEY), D ** -0.5),
        'peer_subkeys': nrm((DEPTH, 2, PEER_NKEYS, PEER_DKEY // 2), (PEER_DKEY // 2) ** -0.5),
        'peer_u': nrm((DEPTH, PEER_NEXP, D), D ** -0.5),
        'peer_v': nrm((DEPTH, PEER_NEXP, D), 0.5),
    }

def reference(x_prompt, x_sample, c, cache_nat_k, cache_nat_v, cache_mla_ckv, cache_mla_krope, c_ctx,
              w_mod, b_mod, norm1, norm2, w_in, na_q_norm, na_k_norm, na_rel_bias, pool_w, pool_scale,
              mla_cq_norm, mla_ckv_norm, mla_w_uq, mla_w_ukv, mla_q_norm, mla_k_norm, w_out,
              peer_wq, peer_subkeys, peer_u, peer_v):
    y_prompt = x_prompt
    y_sample = x_sample
    ks, vs, ckvs, krs = [], [], [], []
    for l in range(DEPTH):
        lp = dict(w_mod=w_mod[l], b_mod=b_mod[l], norm1=norm1[l], norm2=norm2[l], w_in=w_in[l],
                  na_q_norm=na_q_norm[l], na_k_norm=na_k_norm[l], na_rel_bias=na_rel_bias[l],
                  pool_w=pool_w[l], pool_scale=pool_scale[l], mla_cq_norm=mla_cq_norm[l],
                  mla_ckv_norm=mla_ckv_norm[l], mla_w_uq=mla_w_uq[l], mla_w_ukv=mla_w_ukv[l],
                  mla_q_norm=mla_q_norm[l], mla_k_norm=mla_k_norm[l], w_out=w_out[l],
                  peer_wq=peer_wq[l], peer_subkeys=peer_subkeys[l], peer_u=peer_u[l], peer_v=peer_v[l])
        y_prompt, k_l, v_l, ckv_l, kr_l = context_layer(y_prompt, c_ctx, lp)
        ks.append(k_l)
        vs.append(v_l)
        ckvs.append(ckv_l)
        krs.append(kr_l)
        y_sample = latent_layer(y_sample, c, cache_nat_k[:, l], cache_nat_v[:, l],
                                cache_mla_ckv[:, l], cache_mla_krope[:, l], lp)
    new_nat_k = jnp.stack(ks, axis=1)
    new_nat_v = jnp.stack(vs, axis=1)
    new_mla_ckv = jnp.stack(ckvs, axis=1)
    new_mla_krope = jnp.stack(krs, axis=1)
    return (y_prompt, y_sample, new_nat_k, new_nat_v, new_mla_ckv, new_mla_krope)


_drawn_inputs = setup_inputs


def setup_inputs(seed=0):
    import zlib

    import numpy as np

    out = dict(_drawn_inputs(seed))
    spreads = {}
    factors = {'cache_mla_ckv': 4.257,
     'cache_mla_krope': 6.38,
     'na_q_norm': 8.0,
     'na_rel_bias': 6.377,
     'pool_scale': 3.727,
     'mla_cq_norm': 8.0,
     'mla_q_norm': 8.0,
     'mla_k_norm': 8.0}
    for name, (base, spread) in spreads.items():
        noise = np.random.default_rng([zlib.crc32(name.encode()), seed]).standard_normal(out[name].shape)
        drawn = base * np.exp(spread * noise) if base else spread * noise
        out[name] = __import__('jax').numpy.asarray(drawn.astype(out[name].dtype))
    for name, factor in factors.items():
        out[name] = (out[name] * factor).astype(out[name].dtype)
    return out
```

```python
import numpy as np
import concourse.bass as bass
from concourse import mybir
from contextlib import ExitStack

P = 128
D = 1024
KC = D // P
LAYERS = 2
NB = 5
CTX = NB
NKB = NB + 1
GRID_W, ROWS, STRIP = 64, 8, 16
EPS = 1e-6
HEADS = 6
DH = 64
WIDTH = HEADS * DH
WIN_R, WIN_C = 8, 16
POOLS = (2, 4, 8, 16)
POOL_G = 64
POOL_W = POOL_G * len(POOLS)
QK, ROPE, KVR, QR = 96, 32, 128, 256
PH, NKEYS, TOPK = 8, 128, 16
NEXP = NKEYS * NKEYS
NEG = -1e30
RING = 8
SPAN = 3 * STRIP
RB = (2 * WIN_R - 1) * (2 * WIN_C - 1)
RB_PAD = 64

V_BMOD, V_N1, V_N2, V_CQ, V_CTX, V_C, V_END = 0, 48, 56, 64, 66, 74, 82
G_NQ, G_NK, G_MQ, G_MK, G_CKV, G_POOL, G_END = 0, 64, 128, 224, 320, 448, 704

CHUNKS = [("m0", "mod", 0, 512), ("m1", "mod", 512, 512), ("m2", "mod", 1024, 512), ("m3", "mod", 1536, 512),
          ("A", "in", 0, WIDTH), ("B", "in", WIDTH, WIDTH), ("C", "in", 2 * WIDTH, WIDTH),
          ("D", "in", 3 * WIDTH, POOL_W + QR), ("E", "in", 3 * WIDTH + POOL_W + QR, KVR + ROPE),
          ("P0", "pool", 0, 0), ("P1", "pool", 1, 0),
          ("m4", "mod", 2048, 512), ("m5", "mod", 2560, 512), ("m6", "mod", 3072, 512), ("m7", "mod", 3584, 512),
          ("m8", "mod", 4096, 512), ("m9", "mod", 4608, 512), ("o0", "out", 0, 512), ("o1", "out", 512, 512),
          ("m10", "mod", 5120, 512), ("m11", "mod", 5632, 512), ("q0", "q", 0, 512), ("q1", "q", 512, 512)]
SLOTS = 3


def near(n):
    return list(range(max(0, n - 1), min(3, n + 1) + 1))


class Steps:

    def __init__(self, sem, steps):
        self.sem, self.no = sem, {step: i + 1 for i, step in enumerate(steps)}

    def at(self, step):
        return self.no[step]


class Buffers:

    def __init__(self, full, free, uses):
        self.full, self.free, self.n = full, free, len(full)
        self.uses, self.no = uses, {use: i for i, use in enumerate(uses)}

    def slot(self, use):
        return self.no[use] % self.n

    def before(self, use):
        i = self.no[use]
        return self.uses[i - self.n] if i >= self.n else None

    def turn(self, use):
        return self.no[use] // self.n + 1

    def fills(self, use):
        return self.full[self.slot(use)]

    def frees(self, use):
        return self.free[self.slot(use)]

    def filled(self, use):
        return self.fills(use), self.turn(use)

    def freed(self, use):
        return self.frees(use), self.turn(use)


def attention_items():
    return [(kind, b, h) for kind in ("mla", "na") for b in range(NB) for h in range(HEADS)]


def key_blocks(kind, b):
    if b == 0:
        return [0]
    if kind == "mla":
        return [1, 2, 3, 4, CTX]
    return [m + 1 for m in near(b - 1)] + [CTX]


def build(nc, x_prompt, x_sample, c, c_ctx, cache_nat_k, cache_nat_v, cache_mla_ckv, cache_mla_krope,
          w_mod, b_mod, norm1, norm2, w_in, na_q_norm, na_k_norm, rel_bias, pool_w, pool_scale, mla_cq_norm,
          mla_ckv_norm, mla_w_uq, mla_w_ukv, mla_q_norm, mla_k_norm, w_out, peer_wq, peer_subkeys, peer_u,
          peer_v, t_pool, t_pool_prompt, t_rope, t_mask, y_prompt, y_sample, new_k, new_v, new_ckv, new_krope):
    f32, u32, i32 = mybir.dt.float32, mybir.dt.uint32, mybir.dt.int32
    ALU, ACT, AX = mybir.AluOpType, mybir.ActivationFunctionType, mybir.AxisListType

    with ExitStack() as ctx:
        def sb(name, free, dt=f32, parts=P):
            return ctx.enter_context(nc.sbuf_tensor(name, [parts, free], dt))

        sems = {}

        def sem(name):
            if name not in sems:
                sems[name] = ctx.enter_context(nc.semaphore(name))
            return sems[name]

        X = sb("x", NB * D)
        HO = sb("h_or_mixed", NB * D)
        WR = sb("weight_ring", SLOTS * KC * 512)
        QKN = sb("na_qk_or_gates", 3 * NB * P + 3 * NKB * P)
        PR = sb("mla_qkv_or_expert_rows", RING * D + PH * NB * P)
        SC = sb("scratch", 4608)
        GB = sb("bias_or_small_weights", 2304)
        rows = sb("vec_rows", P)
        cols = sb("vec_cols", P)
        gains = sb("gains", G_END)
        poolw = sb("pool_weights", POOL_W)
        ckc = sb("cached_na_k", WIDTH)
        ckvc = sb("cached_ckv", KVR)
        krope = sb("rope_keys", NKB * ROPE)
        sk_raw = sb("subkeys", P)
        skT = sb("subkeys_t", 2 * NKEYS)
        ident = sb("ident", P)
        mpp = sb("prompt_pooling", 4 * P)
        masks = sb("masks", 4 * SPAN)
        sct = sb("silu_cond", 2 * KC)
        AB = sb("mod_cols", 4 * 16)
        abt = sb("mod_tmp", 16)
        half = sb("minus_half", 8)
        stat = sb("stat_sums", 4 * 8)
        stp = sb("stat_biased", 4 * 8)
        rst = sb("stat_rstd", 4 * 8)
        nmax = sb("neg_max", 2)
        rsum = sb("row_sums", 2 * HEADS)
        rinv = sb("inv_sums", HEADS)
        iota_i = sb("iota_i", 16, i32)
        iota = sb("iota", 16)
        idx_all = sb("next_experts", PH * TOPK)
        gate_all = sb("next_gates", PH * TOPK)
        idx_st = sb("experts", 2 * TOPK, u32)
        gate_st = sb("gates", 2 * TOPK)
        dots = sb("dots", 2 * TOPK)
        gel = sb("gelu_dots", 2 * TOPK)
        wgt = sb("expert_weights", 2 * TOPK)

        def xb(b):
            return X[:, b * D:(b + 1) * D]

        def hT(b, k):
            return HO[:, b * D + k * P:b * D + (k + 1) * P]

        mixed = hT

        def wr(q, n=512):
            s = q % SLOTS
            return WR[:, s * KC * 512:(s + 1) * KC * 512].rearrange("p (k n) -> p k n", k=KC)[:, :, 0:n]

        qn_T = QKN[:, 0:3 * NB * P].rearrange("p (j t) -> p j t", j=3)
        kn_T = QKN[:, 3 * NB * P:].rearrange("p (j t) -> p j t", j=3)
        gate_row = QKN[:, 0:4 * D].rearrange("p (g c n) -> p g c n", g=2, c=2)
        o = 0
        qm_T = PR[0:QK, o:o + HEADS * NB * P].rearrange("p (h t) -> p h t", h=HEADS)
        o += HEADS * NB * P
        km_T = PR[0:QK, o:o + HEADS * NKB * P].rearrange("p (h t) -> p h t", h=HEADS)
        o += HEADS * NKB * P
        v_mla = PR[:, o:o + NKB * WIDTH].rearrange("p (b h e) -> p b h e", b=NKB, h=HEADS)
        o += NKB * WIDTH
        v_na = PR[:, o:o + NKB * WIDTH].rearrange("p (b n) -> p b n", b=NKB)
        o += NKB * WIDTH
        lat_T = PR[:, o:o + 256].rearrange("p (k t) -> p k t", k=2)
        ring = PR[:, 0:RING * D].rearrange("p (s n) -> p s n", s=RING)
        pq_T = PR[:, RING * D:].rearrange("p (h t) -> p h t", h=PH)

        pool_in = SC[:, 0:NB * POOL_W].rearrange("p (b n) -> p b n", b=NB)
        sq = SC[:, 1280:1280 + 576]
        qnb = [SC[:, 1856 + 576 * i:1856 + 576 * (i + 1)] for i in range(2)]
        d_T = SC[0:POOL_G, 3008:3008 + 2 * NB * P].rearrange("p (g t) -> p g t", g=2)
        turned = SC[:, 3008:3008 + HEADS * ROPE].rearrange("p (h e) -> p h e", h=HEADS)
        prob = [SC[:, 640 * i:640 * (i + 1)] for i in range(2)]
        prob_T = [SC[:, 1280 + 640 * i:1280 + 640 * (i + 1)].rearrange("p (k q) -> p k q", k=5) for i in range(2)]
        o_T = [SC[:, D * i:D * (i + 1)].rearrange("p (k t) -> p k t", k=KC) for i in range(2)]
        xn = [SC[:, 2048 + D * i:2048 + D * (i + 1)] for i in range(2)]
        gated = SC[:, 4096:4608]
        junk = SC[:, 0:D]
        tk, t_o = {}, D
        for name, n in (("left", 256), ("cand", 256), ("left2", 256), ("hot", 512), ("sv", 32), ("si", 32),
                        ("sif", 32), ("tv", 16), ("tj", 16), ("ab", 32), ("abf", 32), ("pick", 32), ("ex", 16),
                        ("flat", 16), ("nmx", 1), ("sum", 1), ("inv", 1)):
            tk[name] = SC[:, t_o:t_o + n]
            t_o += n
        w_uq = GB[:, 0:1152].rearrange("p (k n) -> p k n", k=2)
        w_ukv = GB[:, 1152:1920]
        ropes = GB[:, 1920:1920 + 256].rearrange("p (b s n) -> p b s n", b=4, s=2)
        bias = GB[:, :].rearrange("p (h r j) -> p h r j", h=HEADS, r=ROWS)

        def pp(name):
            return ctx.enter_context(nc.psum_tensor(name, [P, 2, 512], f32))

        mm, pair, tt = pp("products"), [pp("scores0"), pp("scores1")], pp("transposes")
        tokens = mm[:, :, :].rearrange("p a n -> p (a n)")
        acc = pair[0][:, :, :].rearrange("p a n -> p (a n)")

        items = attention_items()
        ITEMS = len(items)
        CH = {(l, name): l * len(CHUNKS) + i for l in range(LAYERS) for i, (name, *_) in enumerate(CHUNKS)}
        UNITS = NB * PH
        UROWS = 2 * TOPK
        NORMED = NB * 2
        PAIRS_NA = sum(1 for kind, b, h in items if kind == "na" and b)

        def pt_parts(kind, b):
            nk = len(key_blocks(kind, b))
            return [(0, min(nk, 4))] + ([(4, nk)] if nk > 4 else [])

        def pt_engine(item, part):
            return "vector" if item[0] == "mla" and item[1] and part == 0 else "scalar"

        mm_uses, tt_uses, ss_uses, qn_uses, xn_uses, ot_uses, rs_uses, stat_uses = [], [], [], [], [], [], [], []
        for l in range(LAYERS):
            mm_uses += [(k, l, b) for k in "ABCDE" for b in range(NB)]
            mm_uses += [("py", l, g, b) for g in range(2) for b in range(NB)]
            mm_uses += [("pv", l, kind, b) for kind in ("mla", "na") for b in range(NB)]
            mm_uses += [("g", l, 0, j, cnd) for j in range(2) for cnd in range(2)]
            mm_uses += [("o", l, b, j) for b in range(NB) for j in range(2)]
            mm_uses += [("g", l, 1, j, cnd) for j in range(2) for cnd in range(2)]
            mm_uses += [("q", l, h, part) for h in range(PH) for part in range(2)]

            tt_uses += [("vec", l), ("subk", l), ("mc", l, "n1")]
            tt_uses += [("n1", l, b, hf) for b in range(NB) for hf in range(2)]
            tt_uses += [(k, l, b) for k in ("At", "Bt") for b in range(NB)] + [("ct", l)]
            for first, heads_t, n in (("cqt", "qmt", NB), ("ckt", "kmt", NKB)):
                for b in range(1, n + 2):
                    tt_uses += [(first, l, b - 1)] * (b <= n)
                    tt_uses += [(heads_t, l, b - 2, part) for part in range(2)] * (b >= 2)
            tt_uses += [("pt", l, i, part) for i in range(ITEMS) for part in range(len(pt_parts(*items[i][:2])))]
            tt_uses += [("mc", l, "n2")]
            for b in range(NB + 1):
                tt_uses += [("ot", l, b, hf) for hf in range(2)] * (b < NB)
                tt_uses += [("n2", l, b - 1, hf) for hf in range(2)] * (b >= 1)

            ss_uses += [("uq", l, b) for b in range(NB)] + [("ukv", l, b) for b in range(NKB)]
            ss_uses += [(k, l, g) for g in range(2) for k in ("pdp", "pds")]
            ss_uses += [("s", l, i) for i in range(ITEMS)]

            qn_uses += [(k, l, b) for k in "AB" for b in range(NB)]
            for first, second, n in (("D", "uq", NB), ("E", "ukv", NKB)):
                for b in range(n + 1):
                    qn_uses += [(first, l, b)] * (b < NB) + [(second, l, b - 1)] * (b >= 1)
            xn_uses += [(k, l, b) for k in ("n1", "n2") for b in range(NB)]
            ot_uses += [(l, b) for b in range(NB)]
            rs_uses += [(l, kind, b) for kind in ("mla", "na") for b in range(NB)]
            n_qn = len(qn_uses) // (l + 1)
            stat_uses += xn_uses[-2 * NB:-NB] + qn_uses[-n_qn:] + xn_uses[-NB:]

        def family(name, n):
            return [sem(f"{name}{i}") for i in range(n)]

        prods = Buffers(family("products_full", 2), family("products_free", 2), mm_uses)
        flips = Buffers(family("transposes_full", 2), family("transposes_free", 2), tt_uses)
        pairs = Buffers(family("scores_full", 2), family("scores_free", 2), ss_uses)
        qns = Buffers([None] * 2, [None] * 2, qn_uses)
        xns = Buffers([None] * 2, [None] * 2, xn_uses)
        ots = Buffers([None] * 2, [None] * 2, ot_uses)
        rss = Buffers([None] * 2, [None] * 2, rs_uses)
        stats = Buffers(family("sums_ready", 4), [None] * 4, stat_uses)

        def bank(use):
            return mm[:, prods.slot(use), :]

        def tbank(use):
            return tt[:, flips.slot(use), :]

        def sp_(use):
            return pair[pairs.slot(use)]

        def qn(key):
            return qnb[qns.slot(key)]

        def flipped(key):
            k, l, b = key
            return {"A": ("At", l, b), "B": ("Bt", l, b), "D": ("cqt", l, b), "E": ("ckt", l, b),
                    "uq": ("qmt", l, b, 1), "ukv": ("kmt", l, b, 1)}[k]

        def stat_cols(tile, key, n):
            s = 8 * stats.slot(key)
            return tile[:, s:s + n]

        x_in, vectors_in, subkeys_in, gains_in, const_in = (
            sem(n) for n in ("x_in", "vectors_in", "subkeys_in", "gains_in", "const_in"))
        cached_in, cached_v_in, small_in, bias_in = (
            sem(n) for n in ("cached_in", "cached_v_in", "small_in", "bias_in"))
        weights_in = family("weights_in", SLOTS)
        k_out, v_out, latent_out, y_out = (sem(n) for n in ("k_out", "v_out", "latent_out", "y_out"))
        setup = sem("setup")
        ROWS_CLEARED, IDENT_CLEARED, IDENTITY, SKT_CLEARED, IOTA_I, SET_UP = 1, 2, 4, 5, 6, 7
        silu_done = sem("silu_done")
        mod_part = sem("mod_chunks_used")
        mod_ready = sem("mod_cols_ready")
        squares = Steps(sem("squares_ready"), [k for k in qn_uses if k[0] in ("A", "B", "uq", "ukv")])
        stat_biased = sem("stat_biased")
        rstd_ready = Steps(sem("rstd_ready"), stat_uses)
        tokens_scaled = Steps(sem("tokens_scaled"), xn_uses)
        keys_scaled = sem("keys_scaled")
        gained = Steps(sem("gain_applied"), [k for k in qn_uses if k[0] != "D"])
        roped = Steps(sem("roped"), [(k, l, b) for l in range(LAYERS) for k in ("uq", "ukv") for b in range(1, NB)])
        rope_step = sem("rope_step")
        vec_cols, subkeys_ready = sem("vec_cols"), sem("subkeys_turned")
        pool_in_ready, rope_keys = sem("pool_in_ready"), sem("rope_keys_copied")
        values_ready, assembled = sem("mla_values_ready"), sem("keys_assembled")
        bias_added, mask_added = sem("bias_added"), sem("mask_added")
        maxima, inv_ready = sem("maxima_ready"), sem("inv_sums_ready")
        head_attended = sem("head_attended")
        x_updated = Steps(sem("x_updated"), [s for l in range(LAYERS) for s in
                                             [("mixer", l, b, j) for b in range(NB) for j in range(2)]
                                             + [("peer", l, b) for b in range(NB)]])
        tokens_ready, peer_sums = sem("peer_tokens"), sem("peer_sums")
        row_in = family("row_in", RING)
        row_used, idx_ready = sem("rows_used"), sem("experts_ready")
        gelu_ready = sem("gelu_ready")
        top_ready, gexp_ready = sem("top_ready"), sem("gate_exp_ready")
        topk_step, steps_allowed = sem("topk_step"), sem("steps_allowed")
        score_full, score_free = family("peer_scores_full", 2), family("peer_scores_free", 2)

        def chunk_in(q):
            return weights_in[q % SLOTS], 16 * (q // SLOTS + 1)

        def chunk_used(q):
            l, name = q // len(CHUNKS), CHUNKS[q % len(CHUNKS)][0]
            if name in "ABCDE":
                return prods.filled((name, l, NB - 1))
            if name[0] == "P":
                return pairs.filled(("pds", l, int(name[1])))
            if name[0] == "o":
                return prods.filled(("o", l, NB - 1, int(name[1])))
            if name[0] == "q":
                return prods.filled(("q", l, 4 * int(name[1]) + 3, 1))
            if name in ("m4", "m5", "m10", "m11"):
                return prods.filled(("g", l, int(name in ("m10", "m11")), int(name in ("m5", "m11")), 1))
            if name in ("m3", "m9"):
                return flips.filled(("mc", l, "n1" if name == "m3" else "n2"))
            j = int(name[1])
            return mod_part, 6 * l + (j + 1 if j < 3 else j - 6 + 4)

        def rows_scaled(key):
            k, l, b = key
            if k in ("n1", "n2"):
                return tokens_scaled.sem, tokens_scaled.at(key)
            if k == "uq":
                return pairs.freed(key)
            if k == "ukv":
                return keys_scaled, l * NKB + b + 1
            return prods.freed(key)

        def head_done(l, i):
            kind, b, h = items[i]
            if h == HEADS - 1:
                return prods.filled(("pv", l, kind, b))
            return head_attended, l * (ITEMS - ITEMS // HEADS) + (HEADS - 1) * (i // HEADS) + h + 1
        block = ctx.enter_context(nc.Block())

        @block.sync
        def _(sp):
            for b in range(NB):
                sp.dma_start(xb(b), x_prompt if b == 0 else x_sample[(b - 1) * P:b * P, :]).then_inc(x_in, 16)

            def weights(l, names):
                arrays = {"mod": w_mod, "in": w_in, "out": w_out, "q": peer_wq}
                for name, arr, first, n in CHUNKS:
                    if name not in names:
                        continue
                    q = CH[(l, name)]
                    if q >= SLOTS:
                        sp.wait_ge(*chunk_used(q - SLOTS))
                    if arr == "pool":
                        dst, src = wr(q), t_pool[:, 8 * first:8 * first + 8, :]
                    else:
                        dst, src = wr(q, n), arrays[arr][l, :, first:first + n].rearrange("(k p) n -> p k n", p=P)
                    sp.dma_start(dst, src).then_inc(weights_in[q % SLOTS], 16)

            for l in range(LAYERS):
                if l:
                    sp.wait_ge(*prods.freed(("q", l - 1, PH - 1, 1)))
                else:
                    sp.wait_ge(setup, ROWS_CLEARED)
                for a, n, src in ((V_BMOD, 48, b_mod[l]), (V_N1, KC, norm1[l]), (V_N2, KC, norm2[l]),
                                  (V_CQ, 2, mla_cq_norm[l]), (V_CTX, KC, c_ctx), (V_C, KC, c)):
                    sp.dma_start(rows[a:a + n, :], src.rearrange("(j p) -> j p", p=P)).then_inc(vectors_in, 16)
                sp.dma_start(sk_raw[:, :].rearrange("m (p k) -> m p k", p=2),
                             peer_subkeys[l].rearrange("p m k -> m p k")).then_inc(subkeys_in, 16)
                for a, n, src in ((G_NQ, DH, na_q_norm), (G_NK, DH, na_k_norm), (G_MQ, QK, mla_q_norm),
                                  (G_MK, QK, mla_k_norm), (G_CKV, KVR, mla_ckv_norm), (G_POOL, POOL_W, pool_scale)):
                    sp.dma_start(gains[:, a:a + n], src[l].partition_broadcast(P)).then_inc(gains_in, 16)
                if l == 0:
                    sp.dma_start(mpp[:, :], t_pool_prompt).then_inc(const_in, 16)
                    sp.dma_start(masks[:, :], t_mask).then_inc(const_in, 16)
                weights(l, ("m0", "m1", "m2"))
                sp.dma_start(ckc[:, :], cache_nat_k[l]).then_inc(cached_in, 16)
                sp.dma_start(ckvc[:, :], cache_mla_ckv[l]).then_inc(cached_in, 16)
                sp.dma_start(krope[:, CTX * ROPE:], cache_mla_krope[l]).then_inc(cached_in, 16)
                if l:
                    sp.wait_ge(bias_added, l * PAIRS_NA)
                sp.dma_start(w_uq, mla_w_uq[l].rearrange("(k p) n -> p k n", p=P)).then_inc(small_in, 16)
                sp.dma_start(w_ukv, mla_w_ukv[l]).then_inc(small_in, 16)
                sp.dma_start(ropes, t_rope.rearrange("b p (s n) -> p b s n", s=2)).then_inc(small_in, 16)
                sp.dma_start(poolw[0:POOL_G, :].rearrange("c (g d) -> c g d", g=4),
                             pool_w[l].rearrange("g c d -> c g d")).then_inc(small_in, 16)
                weights(l, ("m3", "A", "B", "C"))
                if l:
                    sp.wait_ge(x_updated.sem, x_updated.at(("peer", l - 1, NB - 1)))
                sp.dma_start(v_na[:, CTX, :], cache_nat_v[l]).then_inc(cached_v_in, 16)
                weights(l, ("D",))
                sp.wait_ge(gained.sem, gained.at(("B", l, 0)))
                sp.dma_start(new_k[l], qn(("B", l, 0))[:, 0:WIDTH]).then_inc(k_out, 16)
                weights(l, ("E",))
                sp.wait_ge(*prods.freed(("C", l, 0)))
                sp.dma_start(new_v[l], v_na[:, 0, :]).then_inc(v_out, 16)
                weights(l, ("P0", "P1"))
                sp.wait_ge(gained.sem, gained.at(("E", l, 0)))
                sp.dma_start(new_ckv[l], qn(("E", l, 0))[:, 0:KVR]).then_inc(latent_out, 16)
                sp.dma_start(new_krope[l], krope[:, 0:ROPE]).then_inc(latent_out, 16)
                sp.wait_ge(*pairs.filled(("ukv", l, CTX)))
                sp.wait_ge(roped.sem, roped.at(("ukv", l, NB - 1)))
                for h in range(HEADS):
                    for r in range(ROWS):
                        src = bass.AP(tensor=rel_bias.tensor,
                                      offset=RB_PAD + (l * HEADS + h) * RB + (WIN_R - 1 - r) * (2 * WIN_C - 1) - STRIP,
                                      ap=[[2 * WIN_C - 1, ROWS], [1, STRIP], [1, SPAN]])
                        sp.dma_start(bias[:, h, r, :], src).then_inc(bias_in, 16)
                weights(l, ("m4", "m5", "m6", "m7", "m8", "m9", "o0", "o1", "m10", "m11", "q0", "q1"))
            for b in range(NB):
                sp.wait_ge(x_updated.sem, x_updated.at(("peer", LAYERS - 1, b)))
                sp.dma_start(y_prompt if b == 0 else y_sample[(b - 1) * P:b * P, :], xb(b)).then_inc(y_out, 16)
            sp.wait_ge(y_out, 16 * NB)
            sp.wait_ge(k_out, 16 * LAYERS)
            sp.wait_ge(v_out, 16 * LAYERS)
            sp.wait_ge(latent_out, 32 * LAYERS)

        @block.gpsimd
        def _(pool):
            g = nc.gpsimd
            g.memset(rows[:, :], 0.0).then_inc(setup, 1)
            g.memset(ident[:, :], 0.0).then_inc(setup, 1)
            g.memset(half[:, :], -0.5).then_inc(setup, 1)
            pool.wait_ge(setup, IDENT_CLEARED)
            g.affine_select(out=ident[:, :], in_=ident[:, :], compare_op=ALU.not_equal, fill=1.0,
                            base=0, pattern=[[-1, P]], channel_multiplier=1).then_inc(setup, 1)
            g.memset(skT[:, :], 0.0).then_inc(setup, 1)
            g.iota(iota_i[:, :], [[1, 16]], base=0, channel_multiplier=0).then_inc(setup, 1)
            pool.wait_ge(setup, IOTA_I)
            g.tensor_copy(iota[:, :], iota_i[:, :]).then_inc(setup, 1)

            def rstd(key, n, mul, add):
                pool.wait_ge(*stats.filled(key))
                if stats.before(key):
                    pool.wait_ge(*rows_scaled(stats.before(key)))
                t = rstd_ready.at(key)
                g.tensor_scalar(stat_cols(stp, key, n), stat_cols(stat, key, n), mul, add,
                                ALU.mult, ALU.add).then_inc(stat_biased, 1)
                pool.wait_ge(stat_biased, t)
                g.tensor_tensor(stat_cols(rst, key, n), stat_cols(stp, key, n), half[:, 0:n],
                                ALU.pow).then_inc(rstd_ready.sem, 1)

            def rope(key, done):
                b = key[2]
                v = qn(key).rearrange("p (h e) -> p h e", h=HEADS)[:, :, QK - ROPE:]
                pool.wait_ge(gained.sem, gained.at(key))
                for s in range(2):
                    src = v.rearrange("p h (a s i) -> p h a s i", a=2, s=2)[:, :, :, 1 - s, :]
                    dst = turned.rearrange("p h (a s i) -> p h a s i", a=2, s=2)[:, :, :, s, :]
                    sin = ropes[:, b - 1, 1, :].rearrange("p (a s i) -> p a s i", a=2, s=2)[:, :, s, :]
                    for a in range(2):
                        g.tensor_tensor(dst[:, :, a, :], src[:, :, a, :],
                                        sin[:, a, :].unsqueeze(1).broadcast_to([P, HEADS, ROPE // 4]),
                                        ALU.mult).then_inc(rope_step, 1)
                cos = ropes[:, b - 1, 0, :].unsqueeze(1).broadcast_to([P, HEADS, ROPE])
                pool.wait_ge(rope_step, 5 * done - 1)
                g.tensor_tensor(v, v, cos, ALU.mult).then_inc(rope_step, 1)
                pool.wait_ge(rope_step, 5 * done)
                g.tensor_tensor(v, v, turned, ALU.add).then_inc(roped.sem, 1)
                pool.wait_ge(roped.sem, done)

            for l in range(LAYERS):
                for b in range(NB):
                    rstd(("n1", l, b), 1, 1.0 / D, EPS)
                for b in range(NB):
                    rstd(("A", l, b), HEADS, 1.0, DH * EPS)
                for b in range(NB):
                    rstd(("B", l, b), HEADS, 1.0 / DH, EPS)
                pool.wait_ge(small_in, 64 * (l + 1))
                for b in range(NB + 1):
                    if b < NB:
                        rstd(("D", l, b), 1, 1.0 / QR, EPS)
                    if b >= 1:
                        rstd(("uq", l, b - 1), HEADS, 1.0, QK * EPS)
                        if b >= 2:
                            rope(("uq", l, b - 1), roped.at(("uq", l, b - 1)))
                for b in range(NKB + 1):
                    if b < NB:
                        rstd(("E", l, b), 1, 1.0 / KVR, EPS)
                    if b >= 1:
                        rstd(("ukv", l, b - 1), HEADS, 1.0 / QK, EPS)
                        if 1 <= b - 1 < NB:
                            rope(("ukv", l, b - 1), roped.at(("ukv", l, b - 1)))
                for b in range(NB):
                    rstd(("n2", l, b), 1, 1.0 / D, EPS)
                for b in range(NB):
                    with pool.Fori(0, PH // 2) as it:
                        for e in range(2):
                            pool.wait_ge(idx_ready, it * 2 + (l * UNITS + b * PH + e + 1))
                            for r in range(UROWS):
                                n = e * UROWS + r
                                before = (l * UNITS + b * PH) * UROWS + n
                                pool.wait_ge(row_used, it * (2 * UROWS) + (before + 1))
                                pool.sem_inc(sem("gathers_allowed"), 1)
                                k = e * TOPK + r % TOPK
                                g.indirect_dma_start(
                                    ring[:, n % RING, :], None, peer_u if r < TOPK else peer_v,
                                    bass.IndirectOffsetOnAxis(ap=idx_st[:, k:k + 1], axis=0),
                                ).then_inc(row_in[n % RING], 16)

        @block.scalar
        def _(sc):
            a_ = nc.scalar

            def norm(k, l, b):
                key = (k, l, b)
                if xns.before(key):
                    kb, lb, bb = xns.before(key)
                    sc.wait_ge(*flips.filled((kb, lb, bb, 1)))
                if stats.before(key):
                    sc.wait_ge(rstd_ready.sem, rstd_ready.at(stats.before(key)))
                a_.activation(xn[xns.slot(key)], xb(b), ACT.Square,
                              accum_out=stat_cols(stat, key, 1)).then_inc(stats.fills(key), 1)

            def norm_evac(k, l, b):
                use = (k, l, b, 1)
                cnd, a0 = min(b, 1), 0 if k == "n1" else 32
                sc.wait_ge(*flips.filled(use))
                for j in range(4):
                    kk = 4 + j
                    ga, sh = a0 + 2 * kk + cnd, a0 + 16 + 2 * kk + cnd
                    ins = a_.activation(hT(b, kk), tbank(use)[:, j * P:(j + 1) * P], ACT.Identity,
                                        bias=AB[:, sh:sh + 1], scale=AB[:, ga:ga + 1])
                ins.then_inc(flips.frees(use), 1)

            def squares_free(key):
                i = qn_uses.index(key)
                if i:
                    sc.wait_ge(*stats.filled(qn_uses[i - 1]))

            def square_sum(key, n, src):
                squares_free(key)
                sc.wait_ge(rstd_ready.sem, rstd_ready.at(stats.before(key)))
                sc.wait_ge(*prods.filled(key))
                a_.activation(sq[:, 0:n], src, ACT.Square,
                              accum_out=stat_cols(stat, key, 1)).then_inc(stats.fills(key), 1)

            for l in range(LAYERS):
                if l == 0:
                    sc.wait_ge(vec_cols, 1)
                    a_.activation(sct[:, :], cols[:, V_CTX:V_END], ACT.Silu).then_inc(silu_done, 1)
                for b in range(NB + 1):
                    if b < NB:
                        if b == 0 and l:
                            sc.wait_ge(x_updated.sem, x_updated.at(("peer", l - 1, NB - 1)))
                        elif b == 0:
                            sc.wait_ge(x_in, 16 * NB)
                        norm("n1", l, b)
                    if b == 1:
                        sc.wait_ge(mod_ready, 2 * l + 1)
                    if b >= 1:
                        norm_evac("n1", l, b - 1)
                for ch in "AB":
                    for b in range(NB + 1):
                        if b < NB:
                            use = (ch, l, b)
                            squares_free(use)
                            sc.wait_ge(*prods.filled(use))
                            a_.activation(sq[:, 0:WIDTH], bank(use)[:, 0:WIDTH],
                                          ACT.Square).then_inc(squares.sem, 1)
                        if b >= 1:
                            use = (ch + "t", l, b - 1)
                            sc.wait_ge(*flips.filled(use))
                            a_.activation((qn_T if ch == "A" else kn_T)[:, :, (b - 1) * P:b * P],
                                          tbank(use)[:, 0:3 * P].rearrange("p (j t) -> p j t", j=3),
                                          ACT.Copy).then_inc(flips.frees(use), 1)
                use = ("ct", l)
                sc.wait_ge(*flips.filled(use))
                a_.activation(kn_T[:, :, CTX * P:], tbank(use)[:, 0:3 * P].rearrange("p (j t) -> p j t", j=3),
                              ACT.Copy).then_inc(flips.frees(use), 1)
                for b in range(NB):
                    use = ("C", l, b)
                    sc.wait_ge(*prods.filled(use))
                    a_.activation(v_na[:, b, :], bank(use)[:, 0:WIDTH], ACT.Copy).then_inc(prods.frees(use), 1)

                def heads_evac(name, l, b, dst):
                    for part, (h0, h1) in enumerate(((0, 4), (4, 6))):
                        use = (name, l, b, part)
                        sc.wait_ge(*flips.filled(use))
                        a_.activation(dst[:, h0:h1, b * P:(b + 1) * P],
                                      tbank(use)[0:QK, 0:(h1 - h0) * P].rearrange("p (h t) -> p h t", h=h1 - h0),
                                      ACT.Copy).then_inc(flips.frees(use), 1)

                for b in range(NB + 2):
                    if b < NB:
                        square_sum(("D", l, b), QR, bank(("D", l, b))[:, POOL_W:POOL_W + QR])
                    if 1 <= b <= NB:
                        use, key = ("cqt", l, b - 1), ("uq", l, b - 1)
                        if b > 1:
                            sc.wait_ge(*pairs.filled(("uq", l, b - 2)))
                        elif l:
                            sc.wait_ge(*pairs.filled(("ukv", l - 1, CTX)))
                        sc.wait_ge(*flips.filled(use))
                        for j in range(2):
                            ins = a_.activation(lat_T[:, j, :], tbank(use)[:, j * P:(j + 1) * P], ACT.Copy,
                                                scale=cols[:, V_CQ + j:V_CQ + j + 1])
                        ins.then_inc(flips.frees(use), 1)
                        squares_free(key)
                        sc.wait_ge(*pairs.filled(key))
                        a_.activation(sq.rearrange("p (a n) -> p a n", a=2), sp_(key)[:, :, 0:288],
                                      ACT.Square).then_inc(squares.sem, 1)
                    if b >= 2:
                        heads_evac("qmt", l, b - 2, qm_T)
                for b in range(NKB + 2):
                    if b < NB:
                        square_sum(("E", l, b), KVR, bank(("E", l, b))[:, 0:KVR])
                    if 1 <= b <= NKB:
                        use, key = ("ckt", l, b - 1), ("ukv", l, b - 1)
                        sc.wait_ge(*pairs.filled(("ukv", l, b - 2) if b > 1 else ("uq", l, NB - 1)))
                        sc.wait_ge(*flips.filled(use))
                        a_.activation(lat_T[:, 0, :], tbank(use)[:, 0:P], ACT.Copy).then_inc(flips.frees(use), 1)
                        sc.wait_ge(*pairs.filled(key))
                        v3 = sp_(key)[:, :, 0:WIDTH].rearrange("p a (h e) -> p a h e", h=3)
                        for a in range(2):
                            ins = a_.activation(v_mla[:, b - 1, 3 * a:3 * a + 3, :], v3[:, a, :, DH:], ACT.Copy)
                        ins.then_inc(values_ready, 1)
                        squares_free(key)
                        sc.wait_ge(assembled, l * NKB + b)
                        a_.activation(sq, qn(key), ACT.Square).then_inc(squares.sem, 1)
                    if b >= 2:
                        heads_evac("kmt", l, b - 2, km_T)
                for g in range(2):
                    if g == 1:
                        sc.wait_ge(*prods.filled(("py", l, 0, NB - 1)))
                    else:
                        sc.wait_ge(roped.sem, roped.at(("ukv", l, NB - 1)))
                    use = ("pdp", l, g)
                    sc.wait_ge(*pairs.filled(use))
                    a_.activation(d_T[:, :, 0:P], sp_(use)[0:POOL_G, 0, 0:2 * P].rearrange("p (g t) -> p g t", g=2),
                                  ACT.Copy).then_inc(pairs.frees(use), 1)
                    use = ("pds", l, g)
                    sc.wait_ge(*pairs.filled(use))
                    a_.activation(d_T[:, :, P:], sp_(use)[0:POOL_G, :, :], ACT.Copy).then_inc(pairs.frees(use), 1)
                for i in range(ITEMS + 1):
                    if i < ITEMS:
                        kind, b, h = items[i]
                        n = len(key_blocks(kind, b)) * P
                        use, rkey = ("s", l, i), (l, kind, b)
                        if i == 0:
                            sc.wait_ge(*pairs.filled(("pds", l, 1)))
                        if i >= 2:
                            last = len(pt_parts(*items[i - 2][:2])) - 1
                            sc.wait_ge(*flips.filled(("pt", l, i - 2, last)))
                        if h == 0 and rss.before(rkey):
                            sc.wait_ge(inv_ready, rss.no[rss.before(rkey)] + 1)
                        sc.wait_ge(maxima, l * ITEMS + i + 1)
                        rs = HEADS * rss.slot(rkey) + h
                        a_.activation(prob[i % 2][:, 0:n], sp_(use)[:, :, :].rearrange("p a n -> p (a n)")[:, 0:n],
                                      ACT.Exp, bias=nmax[:, i % 2:i % 2 + 1],
                                      accum_out=rsum[:, rs:rs + 1]).then_inc(pairs.frees(use), 1)
                    if i >= 1:
                        for part, (lo, hi) in enumerate(pt_parts(*items[i - 1][:2])):
                            if pt_engine(items[i - 1], part) == "scalar":
                                use = ("pt", l, i - 1, part)
                                if i >= 3:
                                    sc.wait_ge(*head_done(l, i - 3))
                                sc.wait_ge(*flips.filled(use))
                                a_.activation(prob_T[(i - 1) % 2][:, lo:hi, :],
                                              tbank(use)[:, 0:(hi - lo) * P].rearrange("p (k q) -> p k q", q=P),
                                              ACT.Copy).then_inc(flips.frees(use), 1)

                def gates(which):
                    for j in range(2):
                        for cnd in range(2):
                            use = ("g", l, which, j, cnd)
                            sc.wait_ge(*prods.filled(use))
                            a_.activation(gate_row[:, which, cnd, j * 512:(j + 1) * 512], bank(use),
                                          ACT.Copy).then_inc(prods.frees(use), 1)
                gates(0)
                for b in range(NB + 1):
                    if b < NB:
                        if ots.before((l, b)):
                            lb, bb = ots.before((l, b))
                            sc.wait_ge(*prods.filled(("o", lb, bb, 1)))
                        for part in range(2):
                            use = ("ot", l, b, part)
                            sc.wait_ge(*flips.filled(use))
                            a_.activation(o_T[ots.slot((l, b))][:, 4 * part:4 * part + 4, :],
                                          tbank(use).rearrange("p (k t) -> p k t", k=4),
                                          ACT.Copy).then_inc(flips.frees(use), 1)
                        sc.wait_ge(x_updated.sem, x_updated.at(("mixer", l, b, 1)))
                        norm("n2", l, b)
                    if b == 1:
                        sc.wait_ge(mod_ready, 2 * l + 2)
                    if b >= 1:
                        norm_evac("n2", l, b - 1)
                gates(1)
                sc.wait_ge(v_out, 16 * (l + 1))
                for h in range(PH):
                    for part in range(2):
                        use = ("q", l, h, part)
                        lo, hi = (0, P) if part == 0 else (P, NB * P)
                        sc.wait_ge(*prods.filled(use))
                        a_.activation(pq_T[:, h, lo:hi], bank(use)[:, 0:hi - lo],
                                      ACT.Copy).then_inc(prods.frees(use), 1)

                def gate_exp(unit):
                    sc.wait_ge(top_ready, unit)
                    a_.activation(tk["ex"], tk["tv"], ACT.Exp, bias=tk["nmx"],
                                  accum_out=tk["sum"]).then_inc(gexp_ready, 1)

                with sc.Fori(0, PH // 2) as it:
                    for e in range(2):
                        gate_exp(it * 2 + (l * UNITS + e + 1))
                for b in range(NB):
                    with sc.Fori(0, PH // 2) as it:
                        for e in range(2):
                            sc.wait_ge(row_used, it * (2 * UROWS) + (
                                (l * UNITS + b * PH + e) * UROWS + TOPK + RING))
                            a_.activation(gel[:, e * TOPK:(e + 1) * TOPK], dots[:, e * TOPK:(e + 1) * TOPK],
                                          ACT.Gelu_apprx_tanh).then_inc(gelu_ready, 1)
                            if b + 1 < NB:
                                gate_exp(it * 2 + (l * UNITS + (b + 1) * PH + e + 1))

        @block.vector
        def _(dve):
            v_ = nc.vector

            def heads(ap, n=HEADS):
                return ap.rearrange("p (h e) -> p h e", h=n)

            def mod_cols(l, k):
                use = ("mc", l, k)
                a0, jsh, g0 = (0, 0, V_N1) if k == "n1" else (32, 3 * KC, V_N2)
                dve.wait_ge(*flips.filled(use))
                ps = tbank(use)

                def col(j):
                    return cols[:, j:j + KC].unsqueeze(2).broadcast_to([P, KC, 2])

                def two(ap):
                    return ap.rearrange("p (j c) -> p j c", c=2)
                v_.tensor_tensor(two(AB[:, a0 + 16:a0 + 32]), two(ps[:, 0:16]), col(V_BMOD + jsh), ALU.add)
                v_.tensor_tensor(two(abt[:, :]), two(ps[:, 16:32]), col(V_BMOD + jsh + KC),
                                 ALU.add).then_inc(flips.frees(use), 1)
                dve.wait_ge(*flips.freed(use))
                v_.scalar_tensor_tensor(out=two(AB[:, a0:a0 + 16]), in0=two(abt[:, :]), scalar=1.0,
                                        in1=col(g0), op0=ALU.add, op1=ALU.mult).then_inc(mod_ready, 1)
                dve.wait_ge(mod_ready, 2 * l + (1 if k == "n1" else 2))

            def norm(k, l, b):
                key = (k, l, b)
                dve.wait_ge(rstd_ready.sem, rstd_ready.at(key))
                v_.tensor_scalar(xn[xns.slot(key)], xb(b), stat_cols(rst, key, 1), None,
                                 ALU.mult).then_inc(tokens_scaled.sem, 1)

            def norm_evac(k, l, b):
                use = (k, l, b, 0)
                cnd, a0 = min(b, 1), 0 if k == "n1" else 32
                dve.wait_ge(*flips.filled(use))
                for kk in range(4):
                    ga, sh = a0 + 2 * kk + cnd, a0 + 16 + 2 * kk + cnd
                    ins = v_.tensor_scalar(hT(b, kk), tbank(use)[:, kk * P:(kk + 1) * P],
                                           AB[:, ga:ga + 1], AB[:, sh:sh + 1], ALU.mult, ALU.add)
                ins.then_inc(flips.frees(use), 1)

            def head_sums(key, view):
                dve.wait_ge(squares.sem, squares.at(key))
                if stats.before(key):
                    dve.wait_ge(rstd_ready.sem, rstd_ready.at(stats.before(key)))
                v_.tensor_reduce(stat_cols(stat, key, HEADS), view, AX.X, ALU.add).then_inc(stats.fills(key), 1)

            def qn_free(key):
                if qns.before(key):
                    dve.wait_ge(*flips.filled(flipped(qns.before(key))))

            def per_head(key, dst, src, h0, n):
                r = stat_cols(rst, key, 8)[:, h0:h0 + n]
                return v_.tensor_tensor(dst, src, r.unsqueeze(2).broadcast_to(list(src.shape)), ALU.mult)

            def gain_mul(key, view, g0, n):
                g = gains[:, g0:g0 + n]
                if len(view.shape) == 3:
                    g = g.unsqueeze(1).broadcast_to(list(view.shape))
                v_.tensor_tensor(view, view, g, ALU.mult).then_inc(gained.sem, 1)

            STEPS = 26
            steps = [0]

            def topk_unit(e, layer, first_unit, turn, entry):
                base = steps[0]

                def T(ins):
                    ins.then_inc(topk_step, 1)
                    steps[0] += 1
                    dve.wait_ge(topk_step, turn * (2 * STEPS) + steps[0])
                    dve.sem_inc(steps_allowed, 1)

                dve.wait_ge(score_full[e], turn + (first_unit // 2 + 1))
                dve.sem_inc(steps_allowed, 1)
                for p in range(2):
                    src = pair[1][:, e, p * NKEYS:(p + 1) * NKEYS]
                    left = tk["left"][:, p * NKEYS:(p + 1) * NKEYS]
                    sv, si = tk["sv"][:, 16 * p:16 * p + 16], tk["si"].bitcast(u32)[:, 16 * p:16 * p + 16]
                    T(v_.max(sv[:, 0:8], src))
                    T(v_.max_index(si[:, 0:8], sv[:, 0:8], src))
                    T(v_.match_replace(left, sv[:, 0:8], src, -3.0e38))
                    T(v_.max(sv[:, 8:16], left))
                    T(v_.max_index(si[:, 8:16], sv[:, 8:16], left))
                v_.tensor_copy(tk["sif"], tk["si"].bitcast(u32)).then_inc(score_free[e], 1)
                dve.wait_ge(score_free[e], turn + (first_unit // 2 + 1))
                s0 = tk["sv"][:, 0:16].unsqueeze(2).broadcast_to([P, 16, 16])
                s1 = tk["sv"][:, 16:32].unsqueeze(1).broadcast_to([P, 16, 16])
                T(v_.tensor_tensor(tk["cand"].rearrange("p (a b) -> p a b", a=16), s0, s1, ALU.add))
                tv, tj = tk["tv"], tk["tj"].bitcast(u32)
                T(v_.max(tv[:, 0:8], tk["cand"]))
                T(v_.max_index(tj[:, 0:8], tv[:, 0:8], tk["cand"]))
                T(v_.match_replace(tk["left2"], tv[:, 0:8], tk["cand"], -3.0e38))
                T(v_.max(tv[:, 8:16], tk["left2"]))
                T(v_.max_index(tj[:, 8:16], tv[:, 8:16], tk["left2"]))
                v_.tensor_scalar(tk["nmx"], tv[:, 0:1], -1.0, None, ALU.mult).then_inc(top_ready, 1)
                ab = tk["ab"].bitcast(u32)
                T(v_.tensor_single_scalar(ab[:, 0:16], tj, 4, ALU.logical_shift_right))
                T(v_.tensor_single_scalar(ab[:, 16:32], tj, 15, ALU.bitwise_and))
                T(v_.tensor_copy(tk["abf"], ab))
                hot3 = tk["hot"].rearrange("p (k a) -> p k a", a=16)
                T(v_.tensor_tensor(hot3, tk["abf"].unsqueeze(2).broadcast_to([P, 32, 16]),
                                   iota[:, :].unsqueeze(1).broadcast_to([P, 32, 16]), ALU.is_equal))
                hot4 = tk["hot"].rearrange("p (s k a) -> p s k a", s=2, a=16)
                nums = tk["sif"].rearrange("p (s a) -> p s a", s=2).unsqueeze(2).broadcast_to([P, 2, 16, 16])
                T(v_.tensor_tensor(hot4, hot4, nums, ALU.mult))
                T(v_.tensor_reduce(tk["pick"], hot3, AX.X, ALU.add))
                T(v_.scalar_tensor_tensor(out=tk["flat"], in0=tk["pick"][:, 0:16], scalar=float(NKEYS),
                                          in1=tk["pick"][:, 16:32], op0=ALU.mult, op1=ALU.add))
                T(v_.tensor_scalar(idx_all[:, bass.ds(entry * TOPK, TOPK)], tk["flat"], float(layer * NEXP), None,
                                   ALU.add))
                dve.wait_ge(gexp_ready, turn * 2 + (first_unit + e + 1))
                T(v_.reciprocal(tk["inv"], tk["sum"]))
                T(v_.tensor_scalar(gate_all[:, bass.ds(entry * TOPK, TOPK)], tk["ex"], tk["inv"], None, ALU.mult))
                assert steps[0] - base == STEPS

            def stage(e, entry, unit):
                v_.tensor_copy(gate_st[:, e * TOPK:(e + 1) * TOPK],
                               gate_all[:, bass.ds(entry * TOPK, TOPK)]).then_inc(sem("gates_staged"), 1)
                v_.tensor_copy(idx_st[:, e * TOPK:(e + 1) * TOPK],
                               idx_all[:, bass.ds(entry * TOPK, TOPK)]).then_inc(idx_ready, 1)
                dve.wait_ge(sem("gates_staged"), unit)

            for l in range(LAYERS):
                if l == 0:
                    dve.wait_ge(setup, SET_UP)
                use = ("vec", l)
                dve.wait_ge(*flips.filled(use))
                v_.tensor_copy(cols[:, :], tbank(use)[:, 0:P]).then_inc(flips.frees(use), 1)
                if l == 0:
                    dve.wait_ge(*flips.freed(use))
                    dve.sem_inc(vec_cols, 1)
                use = ("subk", l)
                dve.wait_ge(*flips.filled(use))
                v_.tensor_copy(skT[0:64, 0:NKEYS], tbank(use)[0:64, 0:P])
                v_.tensor_copy(skT[64:P, NKEYS:], tbank(use)[64:P, 0:P]).then_inc(flips.frees(use), 1)
                dve.wait_ge(*flips.freed(("vec", l)))
                mod_cols(l, "n1")
                for b in range(NB + 1):
                    if b < NB:
                        norm("n1", l, b)
                    if b >= 1:
                        norm_evac("n1", l, b - 1)
                dve.wait_ge(gains_in, 96 * (l + 1))
                for ch, g0 in (("A", G_NQ), ("B", G_NK)):
                    for b in range(NB):
                        key = (ch, l, b)
                        rows_ = heads(qn(key)[:, 0:WIDTH])
                        head_sums(key, heads(sq[:, 0:WIDTH]))
                        qn_free(key)
                        if key == ("B", l, 2):
                            dve.wait_ge(k_out, 16 * (l + 1))
                        dve.wait_ge(rstd_ready.sem, rstd_ready.at(key))
                        per_head(key, rows_, heads(bank(key)[:, 0:WIDTH]), 0, HEADS).then_inc(prods.frees(key), 1)
                        dve.wait_ge(*prods.freed(key))
                        gain_mul(key, rows_, g0, DH)
                for b in range(NB + 1):
                    if b < NB:
                        key = ("D", l, b)
                        dve.wait_ge(*stats.filled(key))
                        v_.tensor_copy(pool_in[:, b, :], bank(key)[:, 0:POOL_W]).then_inc(pool_in_ready, 1)
                        qn_free(key)
                        dve.wait_ge(rstd_ready.sem, rstd_ready.at(key))
                        v_.tensor_scalar(qn(key)[:, 0:QR], bank(key)[:, POOL_W:POOL_W + QR], stat_cols(rst, key, 1),
                                         None, ALU.mult).then_inc(prods.frees(key), 1)
                    if b >= 1:
                        key = ("uq", l, b - 1)
                        head_sums(key, heads(sq))
                        q = heads(qn(key))
                        ps = sp_(key)[:, :, 0:288].rearrange("p a (h e) -> p a h e", h=3)
                        qn_free(key)
                        dve.wait_ge(rstd_ready.sem, rstd_ready.at(key))
                        for a in range(2):
                            ins = per_head(key, q[:, 3 * a:3 * a + 3, :], ps[:, a, :, :], 3 * a, 3)
                        ins.then_inc(pairs.frees(key), 1)
                        dve.wait_ge(*pairs.freed(key))
                        gain_mul(key, q, G_MQ, QK)
                dve.wait_ge(cached_in, 48 * (l + 1))
                for b in range(NKB + 1):
                    if b < NB:
                        key = ("E", l, b)
                        dve.wait_ge(*stats.filled(key))
                        v_.tensor_copy(krope[:, b * ROPE:(b + 1) * ROPE],
                                       bank(key)[:, KVR:KVR + ROPE]).then_inc(rope_keys, 1)
                        qn_free(key)
                        dve.wait_ge(rstd_ready.sem, rstd_ready.at(key))
                        v_.tensor_scalar(qn(key)[:, 0:KVR], bank(key)[:, 0:KVR], stat_cols(rst, key, 1),
                                         None, ALU.mult).then_inc(prods.frees(key), 1)
                        dve.wait_ge(*prods.freed(key))
                        gain_mul(key, qn(key)[:, 0:KVR], G_CKV, KVR)
                    if b >= 1:
                        key, before = ("ukv", l, b - 1), qns.before(("ukv", l, b - 1))
                        qn_free(key)
                        if before == ("E", l, 0):
                            dve.wait_ge(latent_out, 32 * (l + 1))
                        km = heads(qn(key))
                        ps = sp_(key)[:, :, 0:WIDTH].rearrange("p a (h e) -> p a h e", h=3)
                        dve.wait_ge(values_ready, l * NKB + b)
                        for a in range(2):
                            ins = v_.tensor_copy(km[:, 3 * a:3 * a + 3, 0:DH], ps[:, a, :, 0:DH])
                        ins.then_inc(pairs.frees(key), 1)
                        if b - 1 < NB:
                            dve.wait_ge(rope_keys, l * NB + b)
                        kr = krope[:, (b - 1) * ROPE:b * ROPE].unsqueeze(1).broadcast_to([P, HEADS, ROPE])
                        v_.tensor_copy(km[:, :, DH:], kr).then_inc(assembled, 1)
                        head_sums(key, heads(sq))
                        dve.wait_ge(assembled, l * NKB + b)
                        dve.wait_ge(rstd_ready.sem, rstd_ready.at(key))
                        per_head(key, km, km, 0, HEADS).then_inc(keys_scaled, 1)
                        dve.wait_ge(keys_scaled, l * NKB + b)
                        gain_mul(key, km, G_MK, QK)
                for g in range(2):
                    for b in range(NB):
                        use = ("py", l, g, b)
                        a0 = WIDTH + 2 * POOL_G * g
                        dve.wait_ge(*prods.filled(use))
                        v_.tensor_tensor(HO[:, b * D + a0:b * D + a0 + 2 * POOL_G], bank(use)[:, 0:2 * POOL_G],
                                         gains[:, G_POOL + 2 * POOL_G * g:G_POOL + 2 * POOL_G * (g + 1)],
                                         ALU.mult).then_inc(prods.frees(use), 1)
                with_bias = l * PAIRS_NA
                for i in range(ITEMS + 3):
                    if i < ITEMS:
                        kind, b, h = items[i]
                        blocks = key_blocks(kind, b)
                        n = len(blocks) * P
                        use = ("s", l, i)
                        dve.wait_ge(*pairs.filled(use))
                        s2 = sp_(use)[:, :, :].rearrange("p a n -> p (a n)")
                        if kind == "na" and b > 0:
                            if b == 1 and h == 0:
                                dve.wait_ge(bias_in, 16 * HEADS * ROWS * (l + 1))
                                dve.wait_ge(const_in, 32)
                            with_bias += 1
                            strips = near(b - 1)
                            first = strips[0] - (b - 1) + 1
                            m = len(strips)
                            loc = s2[:, 0:m * P].rearrange("p (m r j) -> p m r j", m=m, r=ROWS)
                            bv = bass.AP(tensor=GB, offset=h * ROWS * SPAN + SPAN - 1 - STRIP * first,
                                         ap=[[2304, P], [-STRIP, m], [SPAN, ROWS], [-1, STRIP]])
                            v_.tensor_tensor(loc, loc, bv, ALU.add).then_inc(bias_added, 1)
                            mo = (b - 1) * SPAN + STRIP * first
                            mv = masks[:, mo:mo + STRIP * m].rearrange("p (m j) -> p m j", m=m).unsqueeze(2)
                            dve.wait_ge(bias_added, with_bias)
                            v_.tensor_tensor(loc, loc, mv.broadcast_to([P, m, ROWS, STRIP]),
                                             ALU.add).then_inc(mask_added, 1)
                            dve.wait_ge(mask_added, with_bias)
                        if i >= 2:
                            dve.wait_ge(*pairs.freed(("s", l, i - 2)))
                        v_.tensor_reduce(nmax[:, i % 2:i % 2 + 1], s2[:, 0:n], AX.X, ALU.max,
                                         negate=True).then_inc(maxima, 1)
                    if 1 <= i <= ITEMS:
                        for part, (lo, hi) in enumerate(pt_parts(*items[i - 1][:2])):
                            if pt_engine(items[i - 1], part) == "vector":
                                use = ("pt", l, i - 1, part)
                                if i >= 3:
                                    dve.wait_ge(*head_done(l, i - 3))
                                dve.wait_ge(*flips.filled(use))
                                v_.tensor_copy(prob_T[(i - 1) % 2][:, lo:hi, :],
                                               tbank(use)[:, 0:(hi - lo) * P].rearrange("p (k q) -> p k q", q=P)
                                               ).then_inc(flips.frees(use), 1)
                    if i >= 3 and items[i - 3][2] == HEADS - 1:
                        kind, b, h = items[i - 3]
                        use, rkey = ("pv", l, kind, b), (l, kind, b)
                        rs = HEADS * rss.slot(rkey)
                        dve.wait_ge(*prods.filled(use))
                        v_.reciprocal(rinv[:, :], rsum[:, rs:rs + HEADS]).then_inc(inv_ready, 1)
                        dve.wait_ge(inv_ready, rss.no[rkey] + 1)
                        a0 = b * D + (0 if kind == "na" else WIDTH + POOL_W)
                        v_.tensor_tensor(heads(HO[:, a0:a0 + WIDTH]), heads(bank(use)[:, 0:WIDTH]),
                                         rinv[:, :].unsqueeze(2).broadcast_to([P, HEADS, DH]),
                                         ALU.mult).then_inc(prods.frees(use), 1)
                mod_cols(l, "n2")
                for b in range(NB + 1):
                    if b < NB:
                        for j in range(2):
                            use, step = ("o", l, b, j), ("mixer", l, b, j)
                            if b == 0:
                                dve.wait_ge(*prods.freed(("g", l, 0, j, 1)))
                            if j or b:
                                dve.wait_ge(x_updated.sem, x_updated.at(step) - 1)
                            dve.wait_ge(*prods.filled(use))
                            v_.tensor_tensor(gated, bank(use), gate_row[:, 0, min(b, 1), j * 512:(j + 1) * 512],
                                             ALU.mult).then_inc(prods.frees(use), 1)
                            xs = X[:, b * D + j * 512:b * D + (j + 1) * 512]
                            dve.wait_ge(*prods.freed(use))
                            v_.tensor_tensor(xs, xs, gated, ALU.add).then_inc(x_updated.sem, 1)
                        norm("n2", l, b)
                    if b >= 1:
                        norm_evac("n2", l, b - 1)

                u0 = l * UNITS
                if l == 0:
                    dve.sem_inc(row_used, RING)
                dve.wait_ge(*prods.filled(("q", l, PH - 1, 1)))
                with dve.Fori(0, PH // 2) as it:
                    for e in range(2):
                        topk_unit(e, l, u0, it, it * 2 + e)
                steps[0] += 2 * STEPS * (PH // 2 - 1)
                stage(0, 0, u0 + 1)
                dve.wait_ge(*prods.freed(("g", l, 1, 1, 1)))
                for b in range(NB):
                    v_.memset(acc, 0.0).then_inc(peer_sums, 1)
                    dve.wait_ge(peer_sums, 2 * (l * NB + b) + 1)
                    dve.wait_ge(tokens_ready, l * NB + b + 1)
                    r0 = (u0 + b * PH) * UROWS + RING
                    def peer_pair(it, last=False):
                        for e in range(2):
                            unit = u0 + b * PH + e
                            if not (last and e == 1):
                                stage(1 - e, (it * 2 + (e + 1)) % PH, it * 2 + (unit + 2))
                            for r in range(UROWS):
                                n = e * UROWS + r
                                slot_uses = (u0 + b * PH) * UROWS // RING + n // RING
                                dve.wait_ge(row_in[n % RING], it * (16 * 2 * UROWS // RING) + 16 * (slot_uses + 1))
                                if r == TOPK:
                                    dve.wait_ge(gelu_ready, it * 2 + (unit + 1))
                                    mine = slice(e * TOPK, (e + 1) * TOPK)
                                    v_.tensor_tensor(wgt[:, mine], gel[:, mine], gate_st[:, mine],
                                                     ALU.mult).then_inc(sem("expert_weights"), 1)
                                    dve.wait_ge(sem("expert_weights"), it * 2 + (unit + 1))
                                dve.wait_ge(row_used, it * (2 * UROWS) + (r0 + n))
                                row = ring[:, n % RING, :]
                                k = e * TOPK + r % TOPK
                                if r < TOPK:
                                    ins = v_.tensor_tensor_reduce(out=junk, in0=row, in1=tokens, scale=1.0,
                                                                  scalar=0.0, op0=ALU.mult, op1=ALU.add,
                                                                  accum_out=dots[:, k:k + 1])
                                else:
                                    ins = v_.scalar_tensor_tensor(out=acc, in0=row, scalar=wgt[:, k:k + 1], in1=acc,
                                                                  op0=ALU.mult, op1=ALU.add)
                                ins.then_inc(row_used, 1)
                                if r == TOPK - 1 and b + 1 < NB:
                                    topk_unit(e, l, unit - e + PH, it, it * 2 + e)

                    if b + 1 < NB:
                        with dve.Fori(0, PH // 2) as it:
                            peer_pair(it)
                    else:
                        with dve.Fori(0, PH // 2 - 1) as it:
                            peer_pair(it)
                        peer_pair(PH // 2 - 1, last=True)
                    if b + 1 < NB:
                        steps[0] += 2 * STEPS * (PH // 2 - 1)
                    dve.wait_ge(row_used, (u0 + (b + 1) * PH) * UROWS + RING)
                    v_.tensor_tensor(junk, acc, gate_row[:, 1, min(b, 1), :], ALU.mult).then_inc(peer_sums, 1)
                    dve.wait_ge(peer_sums, 2 * (l * NB + b) + 2)
                    v_.tensor_tensor(xb(b), xb(b), junk, ALU.add).then_inc(x_updated.sem, 1)
                    dve.wait_ge(x_updated.sem, x_updated.at(("peer", l, b)))

        @block.tensor
        def _(pe):
            t_ = nc.tensor

            def prod_bank(use):
                if prods.before(use):
                    pe.wait_ge(*prods.freed(prods.before(use)))
                return bank(use)

            def flip_bank(use):
                if flips.before(use):
                    pe.wait_ge(*flips.freed(flips.before(use)))
                return tbank(use)

            def pair_banks(use):
                if pairs.before(use):
                    pe.wait_ge(*pairs.freed(pairs.before(use)))
                return sp_(use)

            def transposes(use, views):
                dst = flip_bank(use)
                for j, v in enumerate(views):
                    n = v.shape[1]
                    ins = t_.transpose(dst[0:n, j * P:(j + 1) * P], v, ident[:, :])
                ins.then_inc(flips.fills(use), 1)

            def block_T(k, l, b):
                x_ = xn[xns.slot((k, l, b))]
                pe.wait_ge(tokens_scaled.sem, tokens_scaled.at((k, l, b)))
                for hf in range(2):
                    transposes((k, l, b, hf), [x_[:, (4 * hf + j) * P:(4 * hf + j + 1) * P] for j in range(4)])

            def heads_T(name, key):
                k, l, b = key
                if 1 <= b < NB:
                    pe.wait_ge(roped.sem, roped.at(key))
                else:
                    pe.wait_ge(gained.sem, gained.at(key))
                rows_ = qn(key).rearrange("p (h e) -> p h e", h=HEADS)
                for part, (h0, h1) in enumerate(((0, 4), (4, 6))):
                    transposes((name, l, b, part), [rows_[:, h, :] for h in range(h0, h1)])

            def mod_columns(l, k, names):
                use = ("mc", l, k)
                dst = flip_bank(use)
                for j, name in enumerate(names):
                    q = CH[(l, name)]
                    w = wr(q)
                    pe.wait_ge(*chunk_in(q))
                    for g in range(4):
                        for kk in range(KC):
                            col = (4 * j + g) * 2
                            ins = t_.matmul(dst[:, col:col + 2], w[:, kk, g * P:(g + 1) * P],
                                            sct[:, :].rearrange("p (c k) -> p k c", c=2)[:, kk, :],
                                            start=kk == 0, stop=kk == KC - 1)
                    ins.then_inc(mod_part if j < 3 else flips.fills(use), 1)

            def gate_rows(l, which, names):
                for j, name in enumerate(names):
                    q = CH[(l, name)]
                    w = wr(q)
                    pe.wait_ge(*chunk_in(q))
                    for cnd in range(2):
                        use = ("g", l, which, j, cnd)
                        dst = prod_bank(use)
                        for g in range(4):
                            row = V_BMOD + (2 if which == 0 else 5) * KC + 4 * j + g
                            out = dst[:, g * P:(g + 1) * P]
                            t_.matmul(out, ident[:, row:row + 1].broadcast_to([P, P]), rows[:, :], start=True,
                                      stop=False)
                            for kk in range(KC):
                                ins = t_.matmul(out, sct[:, cnd * KC + kk:cnd * KC + kk + 1].broadcast_to([P, P]),
                                                w[:, kk, g * P:(g + 1) * P], start=False, stop=kk == KC - 1)
                        ins.then_inc(prods.fills(use), 1)

            def project(name, l, b, n):
                use, q = (name, l, b), CH[(l, name)]
                w, dst = wr(q), prod_bank(use)
                if b == 0:
                    pe.wait_ge(*chunk_in(q))
                if name == "A":
                    pe.wait_ge(*flips.freed(("n1", l, b, 0)))
                    pe.wait_ge(*flips.freed(("n1", l, b, 1)))
                for kk in range(KC):
                    ins = t_.matmul(dst[:, 0:n], hT(b, kk), w[:, kk, 0:n], start=kk == 0, stop=kk == KC - 1)
                ins.then_inc(prods.fills(use), 1)

            for l in range(LAYERS):
                if l == 0:
                    pe.wait_ge(setup, IDENTITY)
                pe.wait_ge(vectors_in, 96 * (l + 1))
                transposes(("vec", l), [rows[:, :]])
                pe.wait_ge(subkeys_in, 16 * (l + 1))
                transposes(("subk", l), [sk_raw[:, :]])
                if l == 0:
                    pe.wait_ge(silu_done, 1)
                mod_columns(l, "n1", ("m0", "m1", "m2", "m3"))
                for b in range(NB):
                    block_T("n1", l, b)
                for ch in "AB":
                    for b in range(NB + 1):
                        if b < NB:
                            project(ch, l, b, WIDTH)
                        if b >= 1:
                            key = (ch, l, b - 1)
                            pe.wait_ge(gained.sem, gained.at(key))
                            transposes((ch + "t", l, b - 1), [qn(key)[:, j * P:(j + 1) * P] for j in range(3)])
                pe.wait_ge(cached_in, 48 * (l + 1))
                transposes(("ct", l), [ckc[:, j * P:(j + 1) * P] for j in range(3)])
                for b in range(NB):
                    project("C", l, b, WIDTH)
                pe.wait_ge(small_in, 64 * (l + 1))
                for b in range(NB + 2):
                    if b < NB:
                        project("D", l, b, POOL_W + QR)
                    if 1 <= b <= NB:
                        key = ("D", l, b - 1)
                        pe.wait_ge(*rows_scaled(key))
                        transposes(("cqt", l, b - 1), [qn(key)[:, j * P:(j + 1) * P] for j in range(2)])
                        use = ("uq", l, b - 1)
                        dst = pair_banks(use)
                        pe.wait_ge(*flips.freed(("cqt", l, b - 1)))
                        for a in range(2):
                            for kk in range(2):
                                ins = t_.matmul(dst[:, a, 0:288], lat_T[:, kk, :], w_uq[:, kk, 288 * a:288 * (a + 1)],
                                                start=kk == 0, stop=kk == 1)
                        ins.then_inc(pairs.fills(use), 1)
                    if b >= 2:
                        heads_T("qmt", ("uq", l, b - 2))
                for b in range(NKB + 2):
                    if b < NB:
                        project("E", l, b, KVR + ROPE)
                    if 1 <= b <= NKB:
                        key = ("E", l, b - 1)
                        if b - 1 < NB:
                            pe.wait_ge(gained.sem, gained.at(key))
                            transposes(("ckt", l, b - 1), [qn(key)[:, 0:KVR]])
                        else:
                            transposes(("ckt", l, b - 1), [ckvc[:, :]])
                        use = ("ukv", l, b - 1)
                        dst = pair_banks(use)
                        pe.wait_ge(*flips.freed(("ckt", l, b - 1)))
                        for a in range(2):
                            ins = t_.matmul(dst[:, a, 0:WIDTH], lat_T[:, 0, :], w_ukv[:, WIDTH * a:WIDTH * (a + 1)],
                                            start=True, stop=True)
                        ins.then_inc(pairs.fills(use), 1)
                    if b >= 2:
                        heads_T("kmt", ("ukv", l, b - 2))
                pe.wait_ge(pool_in_ready, NB * (l + 1))
                pe.wait_ge(const_in, 32)
                for g in range(2):
                    q = CH[(l, f"P{g}")]
                    w = wr(q)
                    use = ("pdp", l, g)
                    dst = pair_banks(use)
                    for i in range(2):
                        wg = 2 * g + i
                        ins = t_.matmul(dst[0:POOL_G, 0, i * P:(i + 1) * P],
                                        pool_in[:, 0, wg * POOL_G:(wg + 1) * POOL_G], mpp[:, wg * P:(wg + 1) * P],
                                        start=True, stop=True)
                    ins.then_inc(pairs.fills(use), 1)
                    use = ("pds", l, g)
                    dst = pair_banks(use)
                    pe.wait_ge(*chunk_in(q))
                    for i in range(2):
                        wg = 2 * g + i
                        for m in range(4):
                            ins = t_.matmul(dst[0:POOL_G, i, :], pool_in[:, 1 + m, wg * POOL_G:(wg + 1) * POOL_G],
                                            w[:, 4 * i + m, :], start=m == 0, stop=m == 3)
                    ins.then_inc(pairs.fills(use), 1)
                    pe.wait_ge(*pairs.freed(("pdp", l, g)))
                    pe.wait_ge(*pairs.freed(("pds", l, g)))
                    for b in range(NB):
                        use = ("py", l, g, b)
                        dst = prod_bank(use)
                        for i in range(2):
                            wg = 2 * g + i
                            ins = t_.matmul(dst[:, i * POOL_G:(i + 1) * POOL_G], d_T[:, i, b * P:(b + 1) * P],
                                            poolw[0:POOL_G, wg * POOL_G:(wg + 1) * POOL_G], start=True, stop=True)
                        ins.then_inc(prods.fills(use), 1)
                pe.wait_ge(*flips.freed(("kmt", l, CTX, 0)))
                pe.wait_ge(*flips.freed(("kmt", l, CTX, 1)))
                pe.wait_ge(values_ready, NKB * (l + 1))
                for i in range(ITEMS + 2):
                    if i < ITEMS:
                        kind, b, h = items[i]
                        blocks = key_blocks(kind, b)
                        use = ("s", l, i)
                        dst = pair_banks(use)
                        if kind == "mla":
                            lhs, keys = qm_T[:, h, b * P:(b + 1) * P], km_T[:, h, :]
                        else:
                            lo = DH * (h % 2)
                            lhs = qn_T[lo:lo + DH, h // 2, b * P:(b + 1) * P]
                            keys = kn_T[lo:lo + DH, h // 2, :]
                        if b == 0:
                            spans = [(0, 0, 0, P)]
                        elif kind == "mla":
                            spans = [(0, 0, P, 4 * P), (1, 0, CTX * P, P)]
                        else:
                            m = len(blocks) - 1
                            spans = [(0, 0, blocks[0] * P, m * P), (0, m * P, CTX * P, P)]
                        for a, col, key0, n in spans:
                            ins = t_.matmul(dst[:, a, col:col + n], lhs, keys[:, key0:key0 + n], start=True, stop=True)
                        ins.then_inc(pairs.fills(use), 1)
                    if 1 <= i <= ITEMS:
                        pe.wait_ge(*pairs.freed(("s", l, i - 1)))
                        for part, (lo, hi) in enumerate(pt_parts(*items[i - 1][:2])):
                            transposes(("pt", l, i - 1, part),
                                       [prob[(i - 1) % 2][:, k * P:(k + 1) * P] for k in range(lo, hi)])
                    if i >= 2:
                        kind, b, h = items[i - 2]
                        use = ("pv", l, kind, b)
                        dst = prod_bank(use) if h == 0 else bank(use)
                        blocks = key_blocks(kind, b)
                        for part in range(len(pt_parts(kind, b))):
                            pe.wait_ge(*flips.freed(("pt", l, i - 2, part)))
                        if kind == "na" and b == 0 and h == 0:
                            pe.wait_ge(cached_v_in, 16 * (l + 1))
                        for k, kb in enumerate(blocks):
                            val = v_mla[:, kb, h, :] if kind == "mla" else v_na[:, kb, h * DH:(h + 1) * DH]
                            ins = t_.matmul(dst[:, h * DH:(h + 1) * DH], prob_T[(i - 2) % 2][:, k, :], val,
                                            start=k == 0, stop=k == len(blocks) - 1)
                        ins.then_inc(prods.fills(use) if h == HEADS - 1 else head_attended, 1)
                gate_rows(l, 0, ("m4", "m5"))
                mod_columns(l, "n2", ("m6", "m7", "m8", "m9"))
                q0, q1 = CH[(l, "o0")], CH[(l, "o1")]
                for b in range(NB + 1):
                    if b < NB:
                        if b == 0:
                            pe.wait_ge(*prods.freed(("pv", l, "na", NB - 1)))
                        for hf in range(2):
                            transposes(("ot", l, b, hf), [mixed(b, 4 * hf + j) for j in range(4)])
                        pe.wait_ge(*flips.freed(("ot", l, b, 0)))
                        pe.wait_ge(*flips.freed(("ot", l, b, 1)))
                        for j, q in enumerate((q0, q1)):
                            use, w = ("o", l, b, j), wr(q)
                            dst = prod_bank(use)
                            if b == 0:
                                pe.wait_ge(*chunk_in(q))
                            for kk in range(KC):
                                ins = t_.matmul(dst, o_T[ots.slot((l, b))][:, kk, :], w[:, kk, :], start=kk == 0,
                                                stop=kk == KC - 1)
                            ins.then_inc(prods.fills(use), 1)
                    if b >= 1:
                        block_T("n2", l, b - 1)
                gate_rows(l, 1, ("m10", "m11"))
                pe.wait_ge(*flips.freed(("n2", l, NB - 1, 0)))
                pe.wait_ge(*flips.freed(("n2", l, NB - 1, 1)))
                h_blocks = HO[:, :].rearrange("p (b k t) -> p b k t", b=NB, k=KC)
                for h in range(PH):
                    q = CH[(l, f"q{h // 4}")]
                    w = wr(q)
                    if h % 4 == 0:
                        pe.wait_ge(*chunk_in(q))
                    for part, (b0, b1) in enumerate(((0, 1), (1, NB))):
                        use = ("q", l, h, part)
                        dst = prod_bank(use)
                        for kk in range(KC):
                            ins = t_.matmul(dst[:, 0:(b1 - b0) * P], w[:, kk, (h % 4) * P:(h % 4 + 1) * P],
                                            h_blocks[:, b0:b1, kk, :], start=kk == 0, stop=kk == KC - 1)
                        ins.then_inc(prods.fills(use), 1)
                for b in range(NB):
                    for h in range(PH):
                        unit = l * UNITS + b * PH + h
                        if b == 0:
                            pe.wait_ge(*prods.freed(("q", l, h, 1)))
                        if unit >= 2:
                            pe.wait_ge(score_free[h % 2], unit // 2)
                        t_.matmul(pair[1][:, h % 2, 0:2 * NKEYS], pq_T[:, h, b * P:(b + 1) * P], skT[:, :],
                                  start=True, stop=True).then_inc(score_full[h % 2], 1)
                    if b == 0:
                        pe.wait_ge(*prods.freed(("q", l, PH - 1, 0)))
                        pe.wait_ge(*prods.freed(("q", l, PH - 1, 1)))
                    else:
                        pe.wait_ge(row_used, (l * UNITS + b * PH - 1) * UROWS + TOPK + RING)
                    for k in range(KC):
                        ins = t_.transpose(mm[:, k // 4, (k % 4) * P:(k % 4 + 1) * P], hT(b, k), ident[:, :])
                    ins.then_inc(tokens_ready, 1)


def _tables():
    def pooling(n):
        t = np.arange(n)
        out = np.zeros((len(POOLS), n, n), np.float32)
        for i, w in enumerate(POOLS):
            lo, hi = np.clip(t - w // 2, 0, n), np.clip(t + (w - w // 2), 0, n)
            inside = (t[:, None] >= lo[None]) & (t[:, None] < hi[None])
            out[i] = inside / (hi - lo)[None].astype(np.float32) - np.eye(n)
        return out
    n = ROWS * GRID_W
    at = (np.arange(ROWS)[None, :, None] * GRID_W + np.arange(4)[:, None, None] * STRIP
          + np.arange(STRIP)[None, None, :]).reshape(-1)
    sample = pooling(n)[:, at][:, :, at]
    sample = sample.reshape(4, 4, P, n).transpose(2, 0, 1, 3).reshape(P, 16, n)
    prompt = pooling(P).transpose(1, 0, 2).reshape(P, 4 * P)
    inv = (10000.0 ** (-np.arange(0, ROPE // 2, 2, dtype=np.float32) / (ROPE // 2))).astype(np.float32)
    ang = [pos.astype(np.float32)[:, None] * inv for pos in (at // GRID_W, at % GRID_W)]
    cos = np.concatenate([np.cos(a) for a in ang for _ in range(2)], 1)
    sin = np.concatenate([s * np.sin(a) for a in ang for s in (-1, 1)], 1)
    rope = np.concatenate([cos, sin], 1).astype(np.float32).reshape(4, P, 2 * ROPE)
    mask = np.zeros((P, 4, SPAN), np.float32)
    for s in range(4):
        q = s * STRIP + np.arange(P) % STRIP
        start = np.clip(q - WIN_C // 2, 0, GRID_W - WIN_C)
        key = (s - 1) * STRIP + np.arange(SPAN)
        ok = (key[None] >= start[:, None]) & (key[None] < start[:, None] + WIN_C)
        mask[:, s] = np.where(ok, 0.0, NEG)
    return (np.ascontiguousarray(sample, np.float32), np.ascontiguousarray(prompt, np.float32), rope,
            mask.reshape(P, 4 * SPAN))


def kernel(**inputs):
    import concourse.bacc as _bacc
    from concourse.bass_utils import run_bass_kernel_spmd as _run

    a = {k: np.asarray(v) for k, v in inputs.items()}
    L = LAYERS
    t_pool, t_pool_prompt, t_rope, t_mask = _tables()

    def strips(x):
        return x.reshape(ROWS, 4, STRIP, D).transpose(1, 0, 2, 3).reshape(4 * P, D)

    rb = a["na_rel_bias"][:, :, ::-1, ::-1].reshape(-1)
    arrays = {
        "x_prompt": a["x_prompt"].reshape(P, D), "x_sample": strips(a["x_sample"]), "c": a["c"].reshape(D),
        "c_ctx": a["c_ctx"].reshape(D), "cache_nat_k": a["cache_nat_k"].reshape(L, P, WIDTH),
        "cache_nat_v": a["cache_nat_v"].reshape(L, P, WIDTH),
        "cache_mla_ckv": a["cache_mla_ckv"].reshape(L, P, KVR),
        "cache_mla_krope": a["cache_mla_krope"].reshape(L, P, ROPE), "w_mod": a["w_mod"], "b_mod": a["b_mod"],
        "norm1": a["norm1"], "norm2": a["norm2"], "w_in": a["w_in"], "na_q_norm": a["na_q_norm"],
        "na_k_norm": a["na_k_norm"],
        "rel_bias": np.concatenate([np.zeros(RB_PAD, rb.dtype), rb, np.zeros(RB_PAD, rb.dtype)]),
        "pool_w": a["pool_w"], "pool_scale": a["pool_scale"], "mla_cq_norm": a["mla_cq_norm"],
        "mla_ckv_norm": a["mla_ckv_norm"], "mla_w_uq": a["mla_w_uq"].reshape(L, QR, HEADS * QK),
        "mla_w_ukv": a["mla_w_ukv"].reshape(L, KVR, HEADS * 2 * DH), "mla_q_norm": a["mla_q_norm"],
        "mla_k_norm": a["mla_k_norm"], "w_out": a["w_out"], "peer_wq": a["peer_wq"],
        "peer_subkeys": a["peer_subkeys"], "peer_u": a["peer_u"].reshape(L * NEXP, D),
        "peer_v": a["peer_v"].reshape(L * NEXP, D), "t_pool": t_pool, "t_pool_prompt": t_pool_prompt,
        "t_rope": t_rope, "t_mask": t_mask,
    }
    outs = {"y_prompt": (P, D), "y_sample": (4 * P, D), "new_k": (L, P, WIDTH), "new_v": (L, P, WIDTH),
            "new_ckv": (L, P, KVR), "new_krope": (L, P, ROPE)}
    nc = _bacc.Bacc("TRN2", target_bir_lowering=False, num_devices=1)
    args, in_map = {}, {}
    for name, x in arrays.items():
        x = np.ascontiguousarray(x)
        in_map[f"in_{name}"] = x
        args[name] = nc.dram_tensor(f"in_{name}", x.shape, mybir.dt.from_np(x.dtype), kind="ExternalInput").ap()
    for name, shape in outs.items():
        args[name] = nc.dram_tensor(f"out_{name}", shape, mybir.dt.float32, kind="ExternalOutput").ap()
    build(nc, **args)
    r = _run(nc, [in_map], core_ids=[0]).results[0]
    y = r["out_y_sample"].reshape(4, ROWS, STRIP, D).transpose(1, 0, 2, 3).reshape(1, ROWS * GRID_W, D)
    return (r["out_y_prompt"].reshape(1, P, D), y, r["out_new_k"].reshape(1, L, P, HEADS, DH),
            r["out_new_v"].reshape(1, L, P, HEADS, DH), r["out_new_ckv"].reshape(1, L, P, KVR),
            r["out_new_krope"].reshape(1, L, P, ROPE))
```

```python
import numpy as np
import concourse.bass as bass
from concourse import mybir
from contextlib import ExitStack

P = 128
D = 1024
KC = D // P
LAYERS = 2
NB = 5
CTX = NB
NKB = NB + 1
GRID_W, ROWS, STRIP = 64, 8, 16
EPS = 1e-6
HEADS = 6
DH = 64
WIDTH = HEADS * DH
WIN_R, WIN_C = 8, 16
POOLS = (2, 4, 8, 16)
POOL_G = 64
POOL_W = POOL_G * len(POOLS)
QK, ROPE, KVR, QR = 96, 32, 128, 256
PH, NKEYS, TOPK = 8, 128, 16
NEXP = NKEYS * NKEYS
NEG = -1e30
URING, RING = 4, 8
SPAN = 3 * STRIP
RB = (2 * WIN_R - 1) * (2 * WIN_C - 1)
RB_PAD = 64

V_BMOD, V_N1, V_N2, V_CQ, V_CTX, V_C, V_END = 0, 48, 56, 64, 66, 74, 82
G_NQ, G_NK, G_MQ, G_MK, G_CKV, G_POOL, G_END = 0, 64, 128, 224, 320, 448, 704

CHUNKS = [("m0", "mod", 0, 512), ("m1", "mod", 512, 512), ("m2", "mod", 1024, 512), ("m3", "mod", 1536, 512),
          ("A", "in", 0, WIDTH), ("B", "in", WIDTH, WIDTH), ("C", "in", 2 * WIDTH, WIDTH),
          ("D", "in", 3 * WIDTH, POOL_W + QR), ("E", "in", 3 * WIDTH + POOL_W + QR, KVR + ROPE),
          ("P0", "pool", 0, 0), ("P1", "pool", 1, 0),
          ("m4", "mod", 2048, 512), ("m5", "mod", 2560, 512), ("m6", "mod", 3072, 512), ("m7", "mod", 3584, 512),
          ("m8", "mod", 4096, 512), ("m9", "mod", 4608, 512), ("o0", "out", 0, 512), ("o1", "out", 512, 512),
          ("q0", "q", 0, 512), ("q1", "q", 512, 512), ("m10", "mod", 5120, 512), ("m11", "mod", 5632, 512)]
SLOTS = 3


BESIDE = {0: [("q", 0, 1), ("q", 1, 1)], 1: [("q", 2, 1), ("q", 3, 1)], 2: [("g", 1, 1, 0), ("g", 1, 1, 1)],
          3: [("q", 4, 1), ("q", 5, 1)], 4: [("q", 6, 1), ("q", 7, 1)]}


def near(n):
    return list(range(max(0, n - 1), min(3, n + 1) + 1))


class Steps:

    def __init__(self, sem, steps):
        self.sem, self.no = sem, {step: i + 1 for i, step in enumerate(steps)}

    def at(self, step):
        return self.no[step]


class Buffers:

    def __init__(self, full, free, uses):
        self.full, self.free, self.n = full, free, len(full)
        self.uses, self.no = uses, {use: i for i, use in enumerate(uses)}

    def slot(self, use):
        return self.no[use] % self.n

    def before(self, use):
        i = self.no[use]
        return self.uses[i - self.n] if i >= self.n else None

    def turn(self, use):
        return self.no[use] // self.n + 1

    def fills(self, use):
        return self.full[self.slot(use)]

    def frees(self, use):
        return self.free[self.slot(use)]

    def filled(self, use):
        return self.fills(use), self.turn(use)

    def freed(self, use):
        return self.frees(use), self.turn(use)


def attention_items():
    return [(kind, b, h) for kind in ("mla", "na") for b in range(NB) for h in range(HEADS)]


def key_blocks(kind, b):
    if b == 0:
        return [0]
    if kind == "mla":
        return [1, 2, 3, 4, CTX]
    return [m + 1 for m in near(b - 1)] + [CTX]


def build(nc, x_prompt, x_sample, c, c_ctx, cache_nat_k, cache_nat_v, cache_mla_ckv, cache_mla_krope,
          w_mod, b_mod, norm1, norm2, w_in, na_q_norm, na_k_norm, rel_bias, pool_w, pool_scale, mla_cq_norm,
          mla_ckv_norm, mla_w_uq, mla_w_ukv, mla_q_norm, mla_k_norm, w_out, peer_wq, peer_subkeys, peer_u,
          peer_v, t_pool, t_pool_prompt, t_rope, t_mask, y_prompt, y_sample, new_k, new_v, new_ckv, new_krope):
    f32, u32, i32 = mybir.dt.float32, mybir.dt.uint32, mybir.dt.int32
    ALU, ACT, AX = mybir.AluOpType, mybir.ActivationFunctionType, mybir.AxisListType

    with ExitStack() as ctx:
        def sb(name, free, dt=f32, parts=P):
            return ctx.enter_context(nc.sbuf_tensor(name, [parts, free], dt))

        sems = {}

        def sem(name):
            if name not in sems:
                sems[name] = ctx.enter_context(nc.semaphore(name))
            return sems[name]

        X = sb("x", NB * D)
        HO = sb("h_or_mixed", NB * D)
        WR = sb("weight_ring", SLOTS * KC * 512)
        QKN = sb("na_qk_or_gates", 3 * NB * P + 3 * NKB * P)
        PR = sb("mla_qkv_or_expert_rows", RING * D + PH * NB * P)
        SC = sb("scratch", 4608)
        GB = sb("bias_or_small_weights", 2304)
        rows = sb("vec_rows", P)
        cols = sb("vec_cols", P)
        gains = sb("gains", G_END)
        poolw = sb("pool_weights", POOL_W)
        ckc = sb("cached_na_k", WIDTH)
        ckvc = sb("cached_ckv", KVR)
        krope = sb("rope_keys", NKB * ROPE)
        sk_raw = sb("subkeys", P)
        skT = sb("subkeys_t", 2 * NKEYS)
        ident = sb("ident", P)
        mpp = sb("prompt_pooling", 4 * P)
        masks = sb("masks", 4 * SPAN)
        sct = sb("silu_cond", 2 * KC)
        AB = sb("mod_cols", 4 * 16)
        abt = sb("mod_tmp", 16)
        half = sb("minus_half", 8)
        stat = sb("stat_sums", 4 * 8)
        stp = sb("stat_biased", 4 * 8)
        rst = sb("stat_rstd", 4 * 8)
        nmax = sb("neg_max", 2)
        rsum = sb("row_sums", 2 * HEADS)
        rinv = sb("inv_sums", HEADS)
        iota_i = sb("iota_i", 16, i32)
        iota = sb("iota", 16)
        idx_next = sb("next_experts", 2 * TOPK)
        gate_next = sb("next_gates", 2 * TOPK)
        diags = sb("weight_diagonals", TOPK * P)
        idx_st = sb("experts", 2 * TOPK, u32)
        gate_st = sb("gates", 2 * TOPK)
        dots = sb("dots", 2 * TOPK)
        gel = sb("gelu_dots", 2 * TOPK)
        wgt = sb("expert_weights", 2 * TOPK)

        def xb(b):
            return X[:, b * D:(b + 1) * D]

        def hT(b, k):
            return HO[:, b * D + k * P:b * D + (k + 1) * P]

        mixed = hT

        def wr(q, n=512):
            s = q % SLOTS
            return WR[:, s * KC * 512:(s + 1) * KC * 512].rearrange("p (k n) -> p k n", k=KC)[:, :, 0:n]

        qn_T = QKN[:, 0:3 * NB * P].rearrange("p (j t) -> p j t", j=3)
        kn_T = QKN[:, 3 * NB * P:].rearrange("p (j t) -> p j t", j=3)
        gate_row = QKN[:, 0:4 * D].rearrange("p (g c n) -> p g c n", g=2, c=2)
        o = 0
        qm_T = PR[0:QK, o:o + HEADS * NB * P].rearrange("p (h t) -> p h t", h=HEADS)
        o += HEADS * NB * P
        km_T = PR[0:QK, o:o + HEADS * NKB * P].rearrange("p (h t) -> p h t", h=HEADS)
        o += HEADS * NKB * P
        v_mla = PR[:, o:o + NKB * WIDTH].rearrange("p (b h e) -> p b h e", b=NKB, h=HEADS)
        o += NKB * WIDTH
        v_na = PR[:, o:o + NKB * WIDTH].rearrange("p (b n) -> p b n", b=NKB)
        o += NKB * WIDTH
        mod_rows = PR[0:2, 0:2 * 512].rearrange("p (s n) -> p s n", s=2)
        lat_T = PR[:, o:o + 256].rearrange("p (k t) -> p k t", k=2)
        v_ring = PR[:, 0:RING * D].rearrange("p (s n) -> p s n", s=RING)
        u_ring = [QKN[:, 0:D], QKN[:, D:2 * D], GB[:, 0:D], GB[:, D:2 * D]]
        pq_T = PR[:, RING * D:].rearrange("p (h t) -> p h t", h=PH)

        pool_in = SC[:, 0:NB * POOL_W].rearrange("p (b n) -> p b n", b=NB)
        sq = SC[:, 1280:1280 + 576]
        qnb = [SC[:, 1856 + 576 * i:1856 + 576 * (i + 1)] for i in range(2)]
        d_T = SC[0:POOL_G, 3008:3008 + 2 * NB * P].rearrange("p (g t) -> p g t", g=2)
        turned = SC[:, 3008:3008 + HEADS * ROPE].rearrange("p (h e) -> p h e", h=HEADS)
        prob = [SC[:, 640 * i:640 * (i + 1)] for i in range(2)]
        prob_T = [SC[:, 1280 + 640 * i:1280 + 640 * (i + 1)].rearrange("p (k q) -> p k q", k=5) for i in range(2)]
        o_T = [SC[:, D * i:D * (i + 1)].rearrange("p (k t) -> p k t", k=KC) for i in range(2)]
        xn = [SC[:, 2048 + D * i:2048 + D * (i + 1)] for i in range(2)]
        gated = SC[:, 4096:4608]
        block_sum = SC[:, 0:D]
        tokens = SC[:, 4608 - D:4608]
        tk, t_o = {}, D
        for name, n in (("scores", 256), ("left", 256), ("cand", 256), ("left2", 256), ("hot", 512), ("sv", 32), ("si", 32),
                        ("sif", 32), ("tv", 16), ("tj", 16), ("ab", 32), ("abf", 32), ("pick", 32), ("ex", 16),
                        ("flat", 16), ("nmx", 1), ("sum", 1), ("inv", 1)):
            tk[name] = SC[:, t_o:t_o + n]
            t_o += n
        assert t_o <= 4608 - D
        w_uq = GB[:, 0:1152].rearrange("p (k n) -> p k n", k=2)
        w_ukv = GB[:, 1152:1920]
        ropes = GB[:, 1920:1920 + 256].rearrange("p (b s n) -> p b s n", b=4, s=2)
        bias = GB[:, :].rearrange("p (h r j) -> p h r j", h=HEADS, r=ROWS)

        def pp(name):
            return ctx.enter_context(nc.psum_tensor(name, [P, 2, 512], f32))

        mm, pair0 = pp("products"), pp("scores0")
        rest = ctx.enter_context(nc.psum_tensor("scores1_transposes", [P, 4, 512], f32))
        pair, tt = [pair0, rest[:, 0:2, :]], rest[:, 2:4, :]
        acc = pair0[:, :, :].rearrange("p a n -> p (a n)")
        key_scores = rest[:, :, :].rearrange("p a n -> p (a n)")

        items = attention_items()
        ITEMS = len(items)
        CH = {(l, name): l * len(CHUNKS) + i for l in range(LAYERS) for i, (name, *_) in enumerate(CHUNKS)}
        UNITS = NB * PH
        PAIRS_NA = sum(1 for kind, b, h in items if kind == "na" and b)

        def pt_parts(kind, b):
            nk = len(key_blocks(kind, b))
            return [(0, min(nk, 4))] + ([(4, nk)] if nk > 4 else [])

        def pt_engine(item, part):
            return "vector" if item[0] == "mla" and item[1] and part == 0 else "scalar"

        mm_uses, tt_uses, ss_uses, qn_uses, xn_uses, ot_uses, rs_uses, stat_uses = [], [], [], [], [], [], [], []
        for l in range(LAYERS):
            mm_uses += [("r", l, m) for m in range(4)]
            mm_uses += [(k, l, b) for k in "ABCDE" for b in range(NB)]
            mm_uses += [("py", l, g, b) for g in range(2) for b in range(NB)]
            mm_uses += [("pv", l, kind, b) for kind in ("mla", "na") for b in range(NB)]
            mm_uses += [("r", l, 4), ("r", l, 5), ("g", l, 0, 0, 0), ("g", l, 0, 0, 1), ("r", l, 6),
                        ("g", l, 0, 1, 0), ("g", l, 0, 1, 1), ("r", l, 7), ("r", l, 8), ("r", l, 9)]
            mm_uses += [("o", l, b, j) for b in range(NB) for j in range(2)]
            mm_uses += [("q", l, h, 0) for h in range(PH)] + [("t", l, 0, hf) for hf in range(2)]
            mm_uses += [("g", l, 1, 0, cnd) for cnd in range(2)]
            mm_uses += [(use[0], l, *use[1:]) for unit in BESIDE for use in BESIDE[unit]]
            mm_uses += [("t", l, b, hf) for b in range(1, NB) for hf in range(2)]

            tt_uses += [("vec", l), ("subk", l), ("mc", l, "n1")]
            tt_uses += [("n1", l, b, hf) for b in range(NB) for hf in range(2)]
            tt_uses += [(k, l, b) for k in ("At", "Bt") for b in range(NB)] + [("ct", l)]
            for first, heads_t, n in (("cqt", "qmt", NB), ("ckt", "kmt", NKB)):
                for b in range(1, n + 2):
                    tt_uses += [(first, l, b - 1)] * (b <= n)
                    tt_uses += [(heads_t, l, b - 2, part) for part in range(2)] * (b >= 2)
            tt_uses += [("pt", l, i, part) for i in range(ITEMS) for part in range(len(pt_parts(*items[i][:2])))]
            tt_uses += [("mc", l, "n2")]
            for b in range(-1, NB + 1):
                tt_uses += [("ot", l, b + 1, hf) for hf in range(2)] * (b + 1 < NB)
                tt_uses += [("n2", l, b - 1, hf) for hf in range(2)] * (b >= 1)

            ss_uses += [("uq", l, b) for b in range(NB)] + [("ukv", l, b) for b in range(NKB)]
            ss_uses += [(k, l, g) for g in range(2) for k in ("pdp", "pds")]
            ss_uses += [("s", l, i) for i in range(ITEMS)]

            qn_uses += [(k, l, b) for k in "AB" for b in range(NB)]
            for first, second, n in (("D", "uq", NB), ("E", "ukv", NKB)):
                for b in range(n + 1):
                    qn_uses += [(first, l, b)] * (b < NB) + [(second, l, b - 1)] * (b >= 1)
            xn_uses += [(k, l, b) for k in ("n1", "n2") for b in range(NB)]
            ot_uses += [(l, b) for b in range(NB)]
            rs_uses += [(l, kind, b) for kind in ("mla", "na") for b in range(NB)]
            n_qn = len(qn_uses) // (l + 1)
            stat_uses += xn_uses[-2 * NB:-NB] + qn_uses[-n_qn:] + xn_uses[-NB:]

        def family(name, n):
            return [sem(f"{name}{i}") for i in range(n)]

        prods = Buffers(family("products_full", 2), family("products_free", 2), mm_uses)
        flips = Buffers(family("transposes_full", 2), family("transposes_free", 2), tt_uses)
        pairs = Buffers(family("scores_full", 2), family("scores_free", 2), ss_uses)
        qns = Buffers([None] * 2, [None] * 2, qn_uses)
        xns = Buffers([None] * 2, [None] * 2, xn_uses)
        ots = Buffers([None] * 2, [None] * 2, ot_uses)
        rss = Buffers([None] * 2, [None] * 2, rs_uses)
        stats = Buffers(family("sums_ready", 4), [None] * 4, stat_uses)

        def bank(use):
            return mm[:, prods.slot(use), :]

        def tbank(use):
            return tt[:, flips.slot(use), :]

        def sp_(use):
            return pair[pairs.slot(use)]

        def qn(key):
            return qnb[qns.slot(key)]

        def flipped(key):
            k, l, b = key
            return {"A": ("At", l, b), "B": ("Bt", l, b), "D": ("cqt", l, b), "E": ("ckt", l, b),
                    "uq": ("qmt", l, b, 1), "ukv": ("kmt", l, b, 1)}[k]

        def stat_cols(tile, key, n):
            s = 8 * stats.slot(key)
            return tile[:, s:s + n]

        x_in, vectors_in, subkeys_in, gains_in, const_in = (
            sem(n) for n in ("x_in", "vectors_in", "subkeys_in", "gains_in", "const_in"))
        cached_in, cached_v_in, small_in, bias_in = (
            sem(n) for n in ("cached_in", "cached_v_in", "small_in", "bias_in"))
        weights_in = family("weights_in", SLOTS)
        k_out, v_out, latent_out, y_out = (sem(n) for n in ("k_out", "v_out", "latent_out", "y_out"))
        setup = sem("setup")
        ROWS_CLEARED, IDENT_CLEARED, IDENTITY, SKT_CLEARED, IOTA_I, SET_UP = 1, 2, 4, 5, 6, 7
        silu_done = sem("silu_done")
        mod_ready = sem("mod_cols_ready")
        squares = Steps(sem("squares_ready"), [k for k in qn_uses if k[0] in ("A", "B", "uq", "ukv")])
        stat_biased = sem("stat_biased")
        rstd_ready = Steps(sem("rstd_ready"), stat_uses)
        tokens_scaled = Steps(sem("tokens_scaled"), xn_uses)
        keys_scaled = sem("keys_scaled")
        gained = Steps(sem("gain_applied"), [k for k in qn_uses if k[0] != "D"])
        roped = Steps(sem("roped"), [(k, l, b) for l in range(LAYERS) for k in ("uq", "ukv") for b in range(1, NB)])
        rope_step = sem("rope_step")
        vec_cols, subkeys_ready = sem("vec_cols"), sem("subkeys_turned")
        pool_in_ready, rope_keys = sem("pool_in_ready"), sem("rope_keys_copied")
        values_ready, assembled = sem("mla_values_ready"), sem("keys_assembled")
        bias_added, mask_added = sem("bias_added"), sem("mask_added")
        maxima, inv_ready = sem("maxima_ready"), sem("inv_sums_ready")
        head_attended = sem("head_attended")
        x_updated = Steps(sem("x_updated"), [s for l in range(LAYERS) for s in
                                             [("mixer", l, b, j) for b in range(NB) for j in range(2)]
                                             + [("peer", l, b) for b in range(NB)]])
        sum_gated = sem("peer_sum_gated")
        u_in, v_in = family("u_row_in", URING), family("v_row_in", RING)
        u_used, v_used = sem("u_rows_used"), sem("v_rows_used")
        idx_ready, gelu_ready, weights_ready = sem("experts_ready"), sem("gelu_ready"), sem("expert_weights_ready")
        gathers_allowed = sem("gathers_allowed")
        gates_staged, diag_ready, sum_copied = sem("gates_staged"), sem("diagonals_ready"), sem("peer_sum_copied")
        top_ready, gexp_ready = sem("top_ready"), sem("gate_exp_ready")
        topk_step, steps_allowed = sem("topk_step"), sem("steps_allowed")
        score_full, score_free = sem("peer_scores_full"), sem("peer_scores_free")

        def chunk_in(q):
            return weights_in[q % SLOTS], 16 * (q // SLOTS + 1)

        def chunk_used(q):
            l, name = q // len(CHUNKS), CHUNKS[q % len(CHUNKS)][0]
            if name in "ABCDE":
                return prods.filled((name, l, NB - 1))
            if name[0] == "P":
                return pairs.filled(("pds", l, int(name[1])))
            if name[0] == "o":
                return prods.filled(("o", l, NB - 1, int(name[1])))
            if name[0] == "q":
                return prods.filled(("q", l, 4 * int(name[1]) + 3, 1))
            if name in ("m10", "m11"):
                return prods.filled(("g", l, 1, int(name == "m11"), 1))
            return prods.filled(("r", l, int(name[1:])))

        def rows_scaled(key):
            k, l, b = key
            if k in ("n1", "n2"):
                return tokens_scaled.sem, tokens_scaled.at(key)
            if k == "uq":
                return pairs.freed(key)
            if k == "ukv":
                return keys_scaled, l * NKB + b + 1
            return prods.freed(key)

        def head_done(l, i):
            kind, b, h = items[i]
            if h == HEADS - 1:
                return prods.filled(("pv", l, kind, b))
            return head_attended, l * (ITEMS - ITEMS // HEADS) + (HEADS - 1) * (i // HEADS) + h + 1
        block = ctx.enter_context(nc.Block())

        @block.sync
        def _(sp):
            for b in range(NB):
                sp.dma_start(xb(b), x_prompt if b == 0 else x_sample[(b - 1) * P:b * P, :]).then_inc(x_in, 16)

            def weights(l, names):
                arrays = {"mod": w_mod, "in": w_in, "out": w_out, "q": peer_wq}
                for name, arr, first, n in CHUNKS:
                    if name not in names:
                        continue
                    q = CH[(l, name)]
                    if q >= SLOTS:
                        sp.wait_ge(*chunk_used(q - SLOTS))
                    if arr == "pool":
                        dst, src = wr(q), t_pool[:, 8 * first:8 * first + 8, :]
                    else:
                        dst, src = wr(q, n), arrays[arr][l, :, first:first + n].rearrange("(k p) n -> p k n", p=P)
                    sp.dma_start(dst, src).then_inc(weights_in[q % SLOTS], 16)

            for l in range(LAYERS):
                if l:
                    sp.wait_ge(*prods.freed(("q", l - 1, PH - 1, 1)))
                else:
                    sp.wait_ge(setup, ROWS_CLEARED)
                for a, n, src in ((V_BMOD, 48, b_mod[l]), (V_N1, KC, norm1[l]), (V_N2, KC, norm2[l]),
                                  (V_CQ, 2, mla_cq_norm[l]), (V_CTX, KC, c_ctx), (V_C, KC, c)):
                    sp.dma_start(rows[a:a + n, :], src.rearrange("(j p) -> j p", p=P)).then_inc(vectors_in, 16)
                sp.dma_start(sk_raw[:, :].rearrange("m (p k) -> m p k", p=2),
                             peer_subkeys[l].rearrange("p m k -> m p k")).then_inc(subkeys_in, 16)
                for a, n, src in ((G_NQ, DH, na_q_norm), (G_NK, DH, na_k_norm), (G_MQ, QK, mla_q_norm),
                                  (G_MK, QK, mla_k_norm), (G_CKV, KVR, mla_ckv_norm), (G_POOL, POOL_W, pool_scale)):
                    sp.dma_start(gains[:, a:a + n], src[l].partition_broadcast(P)).then_inc(gains_in, 16)
                if l == 0:
                    sp.dma_start(mpp[:, :], t_pool_prompt).then_inc(const_in, 16)
                    sp.dma_start(masks[:, :], t_mask).then_inc(const_in, 16)
                weights(l, ("m0", "m1", "m2"))
                sp.dma_start(ckc[:, :], cache_nat_k[l]).then_inc(cached_in, 16)
                sp.dma_start(ckvc[:, :], cache_mla_ckv[l]).then_inc(cached_in, 16)
                sp.dma_start(krope[:, CTX * ROPE:], cache_mla_krope[l]).then_inc(cached_in, 16)
                if l:
                    sp.wait_ge(x_updated.sem, x_updated.at(("peer", l - 1, NB - 1)))
                sp.dma_start(w_uq, mla_w_uq[l].rearrange("(k p) n -> p k n", p=P)).then_inc(small_in, 16)
                sp.dma_start(w_ukv, mla_w_ukv[l]).then_inc(small_in, 16)
                sp.dma_start(ropes, t_rope.rearrange("b p (s n) -> p b s n", s=2)).then_inc(small_in, 16)
                sp.dma_start(poolw[0:POOL_G, :].rearrange("c (g d) -> c g d", g=4),
                             pool_w[l].rearrange("g c d -> c g d")).then_inc(small_in, 16)
                weights(l, ("m3", "A", "B", "C"))
                sp.dma_start(v_na[:, CTX, :], cache_nat_v[l]).then_inc(cached_v_in, 16)
                weights(l, ("D",))
                sp.wait_ge(gained.sem, gained.at(("B", l, 0)))
                sp.dma_start(new_k[l], qn(("B", l, 0))[:, 0:WIDTH]).then_inc(k_out, 16)
                weights(l, ("E",))
                sp.wait_ge(*prods.freed(("C", l, 0)))
                sp.dma_start(new_v[l], v_na[:, 0, :]).then_inc(v_out, 16)
                weights(l, ("P0", "P1"))
                sp.wait_ge(gained.sem, gained.at(("E", l, 0)))
                sp.dma_start(new_ckv[l], qn(("E", l, 0))[:, 0:KVR]).then_inc(latent_out, 16)
                sp.dma_start(new_krope[l], krope[:, 0:ROPE]).then_inc(latent_out, 16)
                sp.wait_ge(*pairs.filled(("ukv", l, CTX)))
                sp.wait_ge(roped.sem, roped.at(("ukv", l, NB - 1)))
                for h in range(HEADS):
                    for r in range(ROWS):
                        src = bass.AP(tensor=rel_bias.tensor,
                                      offset=RB_PAD + (l * HEADS + h) * RB + (WIN_R - 1 - r) * (2 * WIN_C - 1) - STRIP,
                                      ap=[[2 * WIN_C - 1, ROWS], [1, STRIP], [1, SPAN]])
                        sp.dma_start(bias[:, h, r, :], src).then_inc(bias_in, 16)
                weights(l, ("m4", "m5", "m6", "m7", "m8", "m9", "o0", "o1", "q0", "q1", "m10", "m11"))
            for b in range(NB):
                sp.wait_ge(x_updated.sem, x_updated.at(("peer", LAYERS - 1, b)))
                sp.dma_start(y_prompt if b == 0 else y_sample[(b - 1) * P:b * P, :], xb(b)).then_inc(y_out, 16)
            sp.wait_ge(y_out, 16 * NB)
            sp.wait_ge(k_out, 16 * LAYERS)
            sp.wait_ge(v_out, 16 * LAYERS)
            sp.wait_ge(latent_out, 32 * LAYERS)

        @block.gpsimd
        def _(pool):
            g = nc.gpsimd
            g.memset(rows[:, :], 0.0).then_inc(setup, 1)
            g.memset(ident[:, :], 0.0).then_inc(setup, 1)
            g.memset(half[:, :], -0.5).then_inc(setup, 1)
            pool.wait_ge(setup, IDENT_CLEARED)
            g.affine_select(out=ident[:, :], in_=ident[:, :], compare_op=ALU.not_equal, fill=1.0,
                            base=0, pattern=[[-1, P]], channel_multiplier=1).then_inc(setup, 1)
            g.memset(skT[:, :], 0.0).then_inc(setup, 1)
            g.iota(iota_i[:, :], [[1, 16]], base=0, channel_multiplier=0).then_inc(setup, 1)
            pool.wait_ge(setup, IOTA_I)
            g.tensor_copy(iota[:, :], iota_i[:, :]).then_inc(setup, 1)

            def rstd(key, n, mul, add):
                pool.wait_ge(*stats.filled(key))
                if stats.before(key):
                    pool.wait_ge(*rows_scaled(stats.before(key)))
                t = rstd_ready.at(key)
                g.tensor_scalar(stat_cols(stp, key, n), stat_cols(stat, key, n), mul, add,
                                ALU.mult, ALU.add).then_inc(stat_biased, 1)
                pool.wait_ge(stat_biased, t)
                g.tensor_tensor(stat_cols(rst, key, n), stat_cols(stp, key, n), half[:, 0:n],
                                ALU.pow).then_inc(rstd_ready.sem, 1)

            def rope(key, done):
                b = key[2]
                v = qn(key).rearrange("p (h e) -> p h e", h=HEADS)[:, :, QK - ROPE:]
                pool.wait_ge(gained.sem, gained.at(key))
                for s in range(2):
                    src = v.rearrange("p h (a s i) -> p h a s i", a=2, s=2)[:, :, :, 1 - s, :]
                    dst = turned.rearrange("p h (a s i) -> p h a s i", a=2, s=2)[:, :, :, s, :]
                    sin = ropes[:, b - 1, 1, :].rearrange("p (a s i) -> p a s i", a=2, s=2)[:, :, s, :]
                    for a in range(2):
                        g.tensor_tensor(dst[:, :, a, :], src[:, :, a, :],
                                        sin[:, a, :].unsqueeze(1).broadcast_to([P, HEADS, ROPE // 4]),
                                        ALU.mult).then_inc(rope_step, 1)
                cos = ropes[:, b - 1, 0, :].unsqueeze(1).broadcast_to([P, HEADS, ROPE])
                pool.wait_ge(rope_step, 5 * done - 1)
                g.tensor_tensor(v, v, cos, ALU.mult).then_inc(rope_step, 1)
                pool.wait_ge(rope_step, 5 * done)
                g.tensor_tensor(v, v, turned, ALU.add).then_inc(roped.sem, 1)
                pool.wait_ge(roped.sem, done)

            for l in range(LAYERS):
                for b in range(NB):
                    rstd(("n1", l, b), 1, 1.0 / D, EPS)
                for b in range(NB):
                    rstd(("A", l, b), HEADS, 1.0, DH * EPS)
                for b in range(NB):
                    rstd(("B", l, b), HEADS, 1.0 / DH, EPS)
                pool.wait_ge(small_in, 64 * (l + 1))
                for b in range(NB + 1):
                    if b < NB:
                        rstd(("D", l, b), 1, 1.0 / QR, EPS)
                    if b >= 1:
                        rstd(("uq", l, b - 1), HEADS, 1.0, QK * EPS)
                        if b >= 2:
                            rope(("uq", l, b - 1), roped.at(("uq", l, b - 1)))
                for b in range(NKB + 1):
                    if b < NB:
                        rstd(("E", l, b), 1, 1.0 / KVR, EPS)
                    if b >= 1:
                        rstd(("ukv", l, b - 1), HEADS, 1.0 / QK, EPS)
                        if 1 <= b - 1 < NB:
                            rope(("ukv", l, b - 1), roped.at(("ukv", l, b - 1)))
                for b in range(NB):
                    rstd(("n2", l, b), 1, 1.0 / D, EPS)
                for b in range(NB):
                    with pool.Fori(0, PH // 2) as it:
                        for e in range(2):
                            pool.wait_ge(idx_ready, it * 2 + (l * UNITS + b * PH + e + 1))
                            unit = it * 2 + (l * UNITS + b * PH + e)
                            for table, ring, row_in, used in ((peer_u, u_ring, u_in, u_used),
                                                              (peer_v, v_ring, v_in, v_used)):
                                for k in range(TOPK):
                                    pool.wait_ge(used, unit * TOPK + (k + 1))
                                    pool.sem_inc(gathers_allowed, 1)
                                    s = k % len(row_in)
                                    dst = ring[s] if table is peer_u else ring[:, s, :]
                                    g.indirect_dma_start(
                                        dst, None, table,
                                        bass.IndirectOffsetOnAxis(ap=idx_st[:, e * TOPK + k:e * TOPK + k + 1], axis=0),
                                    ).then_inc(row_in[s], 16)

        @block.scalar
        def _(sc):
            a_ = nc.scalar

            def norm(k, l, b):
                key = (k, l, b)
                if xns.before(key):
                    kb, lb, bb = xns.before(key)
                    sc.wait_ge(*flips.filled((kb, lb, bb, 1)))
                if stats.before(key):
                    sc.wait_ge(rstd_ready.sem, rstd_ready.at(stats.before(key)))
                a_.activation(xn[xns.slot(key)], xb(b), ACT.Square,
                              accum_out=stat_cols(stat, key, 1)).then_inc(stats.fills(key), 1)

            def mod_row_evac(l, m):
                use = ("r", l, m)
                sc.wait_ge(*prods.filled(use))
                a_.activation(mod_rows[:, m % 2, :], bank(use)[0:2, :], ACT.Copy).then_inc(prods.frees(use), 1)

            def norm_evac(k, l, b):
                use = (k, l, b, 1)
                cnd, a0 = min(b, 1), 0 if k == "n1" else 32
                sc.wait_ge(*flips.filled(use))
                for j in range(4):
                    kk = 4 + j
                    ga, sh = a0 + 2 * kk + cnd, a0 + 16 + 2 * kk + cnd
                    ins = a_.activation(hT(b, kk), tbank(use)[:, j * P:(j + 1) * P], ACT.Identity,
                                        bias=AB[:, sh:sh + 1], scale=AB[:, ga:ga + 1])
                ins.then_inc(flips.frees(use), 1)

            def squares_free(key):
                i = qn_uses.index(key)
                if i:
                    sc.wait_ge(*stats.filled(qn_uses[i - 1]))

            def square_sum(key, n, src):
                squares_free(key)
                sc.wait_ge(rstd_ready.sem, rstd_ready.at(stats.before(key)))
                sc.wait_ge(*prods.filled(key))
                a_.activation(sq[:, 0:n], src, ACT.Square,
                              accum_out=stat_cols(stat, key, 1)).then_inc(stats.fills(key), 1)

            for l in range(LAYERS):
                if l == 0:
                    sc.wait_ge(vec_cols, 1)
                    a_.activation(sct[:, :], cols[:, V_CTX:V_END], ACT.Silu).then_inc(silu_done, 1)
                for b in range(NB + 1):
                    if b < NB:
                        if b == 0 and l:
                            sc.wait_ge(x_updated.sem, x_updated.at(("peer", l - 1, NB - 1)))
                        elif b == 0:
                            sc.wait_ge(x_in, 16 * NB)
                        norm("n1", l, b)
                    if b == 1:
                        for m in range(4):
                            mod_row_evac(l, m)
                        sc.wait_ge(mod_ready, 2 * l + 1)
                    if b >= 1:
                        norm_evac("n1", l, b - 1)
                for ch in "AB":
                    for b in range(NB + 1):
                        if b < NB:
                            use = (ch, l, b)
                            squares_free(use)
                            sc.wait_ge(*prods.filled(use))
                            a_.activation(sq[:, 0:WIDTH], bank(use)[:, 0:WIDTH],
                                          ACT.Square).then_inc(squares.sem, 1)
                        if b >= 1:
                            use = (ch + "t", l, b - 1)
                            sc.wait_ge(*flips.filled(use))
                            a_.activation((qn_T if ch == "A" else kn_T)[:, :, (b - 1) * P:b * P],
                                          tbank(use)[:, 0:3 * P].rearrange("p (j t) -> p j t", j=3),
                                          ACT.Copy).then_inc(flips.frees(use), 1)
                use = ("ct", l)
                sc.wait_ge(*flips.filled(use))
                a_.activation(kn_T[:, :, CTX * P:], tbank(use)[:, 0:3 * P].rearrange("p (j t) -> p j t", j=3),
                              ACT.Copy).then_inc(flips.frees(use), 1)
                for b in range(NB):
                    use = ("C", l, b)
                    sc.wait_ge(*prods.filled(use))
                    a_.activation(v_na[:, b, :], bank(use)[:, 0:WIDTH], ACT.Copy).then_inc(prods.frees(use), 1)

                def heads_evac(name, l, b, dst):
                    for part, (h0, h1) in enumerate(((0, 4), (4, 6))):
                        use = (name, l, b, part)
                        sc.wait_ge(*flips.filled(use))
                        a_.activation(dst[:, h0:h1, b * P:(b + 1) * P],
                                      tbank(use)[0:QK, 0:(h1 - h0) * P].rearrange("p (h t) -> p h t", h=h1 - h0),
                                      ACT.Copy).then_inc(flips.frees(use), 1)

                for b in range(NB + 2):
                    if b < NB:
                        square_sum(("D", l, b), QR, bank(("D", l, b))[:, POOL_W:POOL_W + QR])
                    if 1 <= b <= NB:
                        use, key = ("cqt", l, b - 1), ("uq", l, b - 1)
                        if b > 1:
                            sc.wait_ge(*pairs.filled(("uq", l, b - 2)))
                        elif l:
                            sc.wait_ge(*pairs.filled(("ukv", l - 1, CTX)))
                        sc.wait_ge(*flips.filled(use))
                        for j in range(2):
                            ins = a_.activation(lat_T[:, j, :], tbank(use)[:, j * P:(j + 1) * P], ACT.Copy,
                                                scale=cols[:, V_CQ + j:V_CQ + j + 1])
                        ins.then_inc(flips.frees(use), 1)
                        squares_free(key)
                        sc.wait_ge(*pairs.filled(key))
                        a_.activation(sq.rearrange("p (a n) -> p a n", a=2), sp_(key)[:, :, 0:288],
                                      ACT.Square).then_inc(squares.sem, 1)
                    if b >= 2:
                        heads_evac("qmt", l, b - 2, qm_T)
                for b in range(NKB + 2):
                    if b < NB:
                        square_sum(("E", l, b), KVR, bank(("E", l, b))[:, 0:KVR])
                    if 1 <= b <= NKB:
                        use, key = ("ckt", l, b - 1), ("ukv", l, b - 1)
                        sc.wait_ge(*pairs.filled(("ukv", l, b - 2) if b > 1 else ("uq", l, NB - 1)))
                        sc.wait_ge(*flips.filled(use))
                        a_.activation(lat_T[:, 0, :], tbank(use)[:, 0:P], ACT.Copy).then_inc(flips.frees(use), 1)
                        sc.wait_ge(*pairs.filled(key))
                        v3 = sp_(key)[:, :, 0:WIDTH].rearrange("p a (h e) -> p a h e", h=3)
                        for a in range(2):
                            ins = a_.activation(v_mla[:, b - 1, 3 * a:3 * a + 3, :], v3[:, a, :, DH:], ACT.Copy)
                        ins.then_inc(values_ready, 1)
                        squares_free(key)
                        sc.wait_ge(assembled, l * NKB + b)
                        a_.activation(sq, qn(key), ACT.Square).then_inc(squares.sem, 1)
                    if b >= 2:
                        heads_evac("kmt", l, b - 2, km_T)
                for g in range(2):
                    if g == 1:
                        sc.wait_ge(*prods.filled(("py", l, 0, NB - 1)))
                    else:
                        sc.wait_ge(roped.sem, roped.at(("ukv", l, NB - 1)))
                    use = ("pdp", l, g)
                    sc.wait_ge(*pairs.filled(use))
                    a_.activation(d_T[:, :, 0:P], sp_(use)[0:POOL_G, 0, 0:2 * P].rearrange("p (g t) -> p g t", g=2),
                                  ACT.Copy).then_inc(pairs.frees(use), 1)
                    use = ("pds", l, g)
                    sc.wait_ge(*pairs.filled(use))
                    a_.activation(d_T[:, :, P:], sp_(use)[0:POOL_G, :, :], ACT.Copy).then_inc(pairs.frees(use), 1)
                for i in range(ITEMS + 1):
                    if i < ITEMS:
                        kind, b, h = items[i]
                        n = len(key_blocks(kind, b)) * P
                        use, rkey = ("s", l, i), (l, kind, b)
                        if i == 0:
                            sc.wait_ge(*pairs.filled(("pds", l, 1)))
                        if i >= 2:
                            last = len(pt_parts(*items[i - 2][:2])) - 1
                            sc.wait_ge(*flips.filled(("pt", l, i - 2, last)))
                        if h == 0 and rss.before(rkey):
                            sc.wait_ge(inv_ready, rss.no[rss.before(rkey)] + 1)
                        sc.wait_ge(maxima, l * ITEMS + i + 1)
                        rs = HEADS * rss.slot(rkey) + h
                        a_.activation(prob[i % 2][:, 0:n], sp_(use)[:, :, :].rearrange("p a n -> p (a n)")[:, 0:n],
                                      ACT.Exp, bias=nmax[:, i % 2:i % 2 + 1],
                                      accum_out=rsum[:, rs:rs + 1]).then_inc(pairs.frees(use), 1)
                    if i >= 1:
                        for part, (lo, hi) in enumerate(pt_parts(*items[i - 1][:2])):
                            if pt_engine(items[i - 1], part) == "scalar":
                                use = ("pt", l, i - 1, part)
                                if i >= 3:
                                    sc.wait_ge(*head_done(l, i - 3))
                                sc.wait_ge(*flips.filled(use))
                                a_.activation(prob_T[(i - 1) % 2][:, lo:hi, :],
                                              tbank(use)[:, 0:(hi - lo) * P].rearrange("p (k q) -> p k q", q=P),
                                              ACT.Copy).then_inc(flips.frees(use), 1)

                def gate_row_evac(which, j, cnd):
                    use = ("g", l, which, j, cnd)
                    sc.wait_ge(*prods.filled(use))
                    a_.activation(gate_row[:, which, cnd, j * 512:(j + 1) * 512], bank(use),
                                  ACT.Copy).then_inc(prods.frees(use), 1)
                mod_row_evac(l, 4)
                mod_row_evac(l, 5)
                for j in range(2):
                    for cnd in range(2):
                        gate_row_evac(0, j, cnd)
                    mod_row_evac(l, 6 + j)
                mod_row_evac(l, 8)
                mod_row_evac(l, 9)
                for b in range(-1, NB + 1):
                    if b + 1 < NB:
                        if ots.before((l, b + 1)):
                            lb, bb = ots.before((l, b + 1))
                            sc.wait_ge(*prods.filled(("o", lb, bb, 1)))
                        for part in range(2):
                            use = ("ot", l, b + 1, part)
                            sc.wait_ge(*flips.filled(use))
                            a_.activation(o_T[ots.slot((l, b + 1))][:, 4 * part:4 * part + 4, :],
                                          tbank(use).rearrange("p (k t) -> p k t", k=4),
                                          ACT.Copy).then_inc(flips.frees(use), 1)
                    if 0 <= b < NB:
                        sc.wait_ge(x_updated.sem, x_updated.at(("mixer", l, b, 1)))
                        norm("n2", l, b)
                    if b == 1:
                        sc.wait_ge(mod_ready, 2 * l + 2)
                    if b >= 1:
                        norm_evac("n2", l, b - 1)
                sc.wait_ge(v_out, 16 * (l + 1))

                def queries_evac(h, part):
                    use = ("q", l, h, part)
                    lo, hi = (0, P) if part == 0 else (P, NB * P)
                    sc.wait_ge(*prods.filled(use))
                    a_.activation(pq_T[:, h, lo:hi], bank(use)[:, 0:hi - lo], ACT.Copy).then_inc(prods.frees(use), 1)

                def tokens_evac(b):
                    for hf in range(2):
                        use = ("t", l, b, hf)
                        sc.wait_ge(*prods.filled(use))
                        a_.activation(tokens[:, hf * 512:(hf + 1) * 512], bank(use),
                                      ACT.Copy).then_inc(prods.frees(use), 1)

                for h in range(PH):
                    queries_evac(h, 0)
                tokens_evac(0)

                def gate_exp(unit):
                    sc.wait_ge(top_ready, unit)
                    a_.activation(tk["ex"], tk["tv"], ACT.Exp, bias=tk["nmx"],
                                  accum_out=tk["sum"]).then_inc(gexp_ready, 1)

                def peer_unit(unit, e, ahead=True, tokens_of=0):
                    sc.wait_ge(u_used, unit * TOPK + (TOPK + URING))
                    a_.activation(gel[:, e * TOPK:(e + 1) * TOPK], dots[:, e * TOPK:(e + 1) * TOPK],
                                  ACT.Gelu_apprx_tanh).then_inc(gelu_ready, 1)
                    if tokens_of:
                        tokens_evac(tokens_of)
                    sc.wait_ge(v_used, unit * TOPK + RING)
                    sc.wait_ge(weights_ready, unit + 1)
                    for k in range(TOPK):
                        w = e * TOPK + k
                        a_.activation(diags[:, k * P:(k + 1) * P], ident[:, :], ACT.Copy,
                                      scale=wgt[:, w:w + 1]).then_inc(diag_ready, 1)
                    if ahead:
                        gate_exp(unit + 3)

                for unit in range(2):
                    gate_exp(l * UNITS + unit + 1)
                    gate_row_evac(1, 0, unit)
                for b in range(NB):
                    u0 = l * UNITS + b * PH
                    if b == 0:
                        for unit in range(PH - 2):
                            peer_unit(u0 + unit, unit % 2)
                            for use in BESIDE.get(unit, []):
                                if use[0] == "q":
                                    queries_evac(*use[1:])
                                else:
                                    gate_row_evac(*use[1:])
                    else:
                        with sc.Fori(0, PH // 2 - 1) as it:
                            for e in range(2):
                                peer_unit(it * 2 + (u0 + e), e)
                    peer_unit(u0 + PH - 2, 0, ahead=b + 1 < NB)
                    peer_unit(u0 + PH - 1, 1, ahead=b + 1 < NB, tokens_of=b + 1 if b + 1 < NB else 0)
                    if b:
                        sc.wait_ge(x_updated.sem, x_updated.at(("peer", l, b - 1)))
                    sc.wait_ge(v_used, (l * UNITS + (b + 1) * PH) * TOPK + RING)
                    a_.activation(block_sum, acc, ACT.Copy).then_inc(sum_copied, 1)

        @block.vector
        def _(dve):
            v_ = nc.vector

            def heads(ap, n=HEADS):
                return ap.rearrange("p (h e) -> p h e", h=n)

            def mod_cols(l, k):
                use = ("mc", l, k)
                a0, jsh, g0 = (0, 0, V_N1) if k == "n1" else (32, 3 * KC, V_N2)
                dve.wait_ge(*flips.filled(use))
                ps = tbank(use)

                def col(j):
                    return cols[:, j:j + KC].unsqueeze(2).broadcast_to([P, KC, 2])

                def two(ap):
                    return ap.rearrange("p (j c) -> p j c", c=2)
                v_.tensor_tensor(two(AB[:, a0 + 16:a0 + 32]), two(ps[:, 0:16]), col(V_BMOD + jsh), ALU.add)
                v_.tensor_tensor(two(abt[:, :]), two(ps[:, 16:32]), col(V_BMOD + jsh + KC),
                                 ALU.add).then_inc(flips.frees(use), 1)
                dve.wait_ge(*flips.freed(use))
                v_.scalar_tensor_tensor(out=two(AB[:, a0:a0 + 16]), in0=two(abt[:, :]), scalar=1.0,
                                        in1=col(g0), op0=ALU.add, op1=ALU.mult).then_inc(mod_ready, 1)
                dve.wait_ge(mod_ready, 2 * l + (1 if k == "n1" else 2))

            def norm(k, l, b):
                key = (k, l, b)
                dve.wait_ge(rstd_ready.sem, rstd_ready.at(key))
                v_.tensor_scalar(xn[xns.slot(key)], xb(b), stat_cols(rst, key, 1), None,
                                 ALU.mult).then_inc(tokens_scaled.sem, 1)

            def norm_evac(k, l, b):
                use = (k, l, b, 0)
                cnd, a0 = min(b, 1), 0 if k == "n1" else 32
                dve.wait_ge(*flips.filled(use))
                for kk in range(4):
                    ga, sh = a0 + 2 * kk + cnd, a0 + 16 + 2 * kk + cnd
                    ins = v_.tensor_scalar(hT(b, kk), tbank(use)[:, kk * P:(kk + 1) * P],
                                           AB[:, ga:ga + 1], AB[:, sh:sh + 1], ALU.mult, ALU.add)
                ins.then_inc(flips.frees(use), 1)

            def head_sums(key, view):
                dve.wait_ge(squares.sem, squares.at(key))
                if stats.before(key):
                    dve.wait_ge(rstd_ready.sem, rstd_ready.at(stats.before(key)))
                v_.tensor_reduce(stat_cols(stat, key, HEADS), view, AX.X, ALU.add).then_inc(stats.fills(key), 1)

            def qn_free(key):
                if qns.before(key):
                    dve.wait_ge(*flips.filled(flipped(qns.before(key))))

            def per_head(key, dst, src, h0, n):
                r = stat_cols(rst, key, 8)[:, h0:h0 + n]
                return v_.tensor_tensor(dst, src, r.unsqueeze(2).broadcast_to(list(src.shape)), ALU.mult)

            def gain_mul(key, view, g0, n):
                g = gains[:, g0:g0 + n]
                if len(view.shape) == 3:
                    g = g.unsqueeze(1).broadcast_to(list(view.shape))
                v_.tensor_tensor(view, view, g, ALU.mult).then_inc(gained.sem, 1)

            STEPS = 16

            def topk_unit(e, layer, unit, turn, head):
                done = [0]

                def step(ins, waited=True, fence=False):
                    ins.then_inc(topk_step, 1)
                    done[0] += 1
                    if waited:
                        dve.wait_ge(topk_step, unit * STEPS + done[0])
                    if fence:
                        dve.sem_inc(steps_allowed, 1)

                dve.wait_ge(score_full, unit + 1)
                v_.tensor_copy(tk["scores"], key_scores[:, bass.ds(head * (2 * NKEYS), 2 * NKEYS)]
                               ).then_inc(score_free, 1)
                dve.wait_ge(score_free, unit + 1)
                dve.sem_inc(steps_allowed, 1)
                src = [tk["scores"][:, p * NKEYS:(p + 1) * NKEYS] for p in range(2)]
                left = [tk["left"][:, p * NKEYS:(p + 1) * NKEYS] for p in range(2)]
                sv = [tk["sv"][:, 16 * p:16 * p + 16] for p in range(2)]
                si = [tk["si"].bitcast(u32)[:, 16 * p:16 * p + 16] for p in range(2)]
                v_.max(sv[0][:, 0:8], src[0])
                step(v_.max(sv[1][:, 0:8], src[1]), fence=True)
                for p in range(2):
                    v_.match_replace(left[p], sv[p][:, 0:8], src[p], -3.0e38)
                v_.max_index(si[0][:, 0:8], sv[0][:, 0:8], src[0])
                step(v_.max_index(si[1][:, 0:8], sv[1][:, 0:8], src[1]), fence=True)
                v_.max(sv[0][:, 8:16], left[0])
                step(v_.max(sv[1][:, 8:16], left[1]), fence=True)
                v_.max_index(si[0][:, 8:16], sv[0][:, 8:16], left[0])
                v_.max_index(si[1][:, 8:16], sv[1][:, 8:16], left[1])
                s0 = tk["sv"][:, 0:16].unsqueeze(2).broadcast_to([P, 16, 16])
                s1 = tk["sv"][:, 16:32].unsqueeze(1).broadcast_to([P, 16, 16])
                step(v_.tensor_tensor(tk["cand"].rearrange("p (a b) -> p a b", a=16), s0, s1, ALU.add), fence=True)
                tv, tj = tk["tv"], tk["tj"].bitcast(u32)
                step(v_.max(tv[:, 0:8], tk["cand"]), fence=True)
                v_.match_replace(tk["left2"], tv[:, 0:8], tk["cand"], -3.0e38)
                v_.max_index(tj[:, 0:8], tv[:, 0:8], tk["cand"])
                step(v_.tensor_copy(tk["sif"], tk["si"].bitcast(u32)), fence=True)
                step(v_.max(tv[:, 8:16], tk["left2"]), fence=True)
                v_.max_index(tj[:, 8:16], tv[:, 8:16], tk["left2"])
                v_.tensor_scalar(tk["nmx"], tv[:, 0:1], -1.0, None, ALU.mult).then_inc(top_ready, 1)
                dve.wait_ge(top_ready, unit + 1)
                ab = tk["ab"].bitcast(u32)
                v_.tensor_single_scalar(ab[:, 0:16], tj, 4, ALU.logical_shift_right)
                step(v_.tensor_single_scalar(ab[:, 16:32], tj, 15, ALU.bitwise_and))
                step(v_.tensor_copy(tk["abf"], ab))
                hot3 = tk["hot"].rearrange("p (k a) -> p k a", a=16)
                step(v_.tensor_tensor(hot3, tk["abf"].unsqueeze(2).broadcast_to([P, 32, 16]),
                                      iota[:, :].unsqueeze(1).broadcast_to([P, 32, 16]), ALU.is_equal))
                hot4 = tk["hot"].rearrange("p (s k a) -> p s k a", s=2, a=16)
                nums = tk["sif"].rearrange("p (s a) -> p s a", s=2).unsqueeze(2).broadcast_to([P, 2, 16, 16])
                step(v_.tensor_tensor(hot4, hot4, nums, ALU.mult))
                step(v_.tensor_reduce(tk["pick"], hot3, AX.X, ALU.add))
                step(v_.scalar_tensor_tensor(out=tk["flat"], in0=tk["pick"][:, 0:16], scalar=float(NKEYS),
                                             in1=tk["pick"][:, 16:32], op0=ALU.mult, op1=ALU.add))
                step(v_.tensor_scalar(idx_next[:, e * TOPK:(e + 1) * TOPK], tk["flat"], float(layer * NEXP), None,
                                      ALU.add), waited=False)
                dve.wait_ge(gexp_ready, unit + 1)
                step(v_.reciprocal(tk["inv"], tk["sum"]))
                step(v_.tensor_scalar(gate_next[:, e * TOPK:(e + 1) * TOPK], tk["ex"], tk["inv"], None, ALU.mult))
                assert done[0] == STEPS, done

            def stage(e, unit):
                mine = slice(e * TOPK, (e + 1) * TOPK)
                v_.tensor_copy(gate_st[:, mine], gate_next[:, mine]).then_inc(gates_staged, 1)
                v_.tensor_copy(idx_st[:, mine], idx_next[:, mine]).then_inc(idx_ready, 1)

            for l in range(LAYERS):
                if l == 0:
                    dve.wait_ge(setup, SET_UP)
                use = ("vec", l)
                dve.wait_ge(*flips.filled(use))
                v_.tensor_copy(cols[:, :], tbank(use)[:, 0:P]).then_inc(flips.frees(use), 1)
                if l == 0:
                    dve.wait_ge(*flips.freed(use))
                    dve.sem_inc(vec_cols, 1)
                use = ("subk", l)
                dve.wait_ge(*flips.filled(use))
                v_.tensor_copy(skT[0:64, 0:NKEYS], tbank(use)[0:64, 0:P])
                v_.tensor_copy(skT[64:P, NKEYS:], tbank(use)[64:P, 0:P]).then_inc(flips.frees(use), 1)
                dve.wait_ge(*flips.freed(("vec", l)))
                mod_cols(l, "n1")
                for b in range(NB + 1):
                    if b < NB:
                        norm("n1", l, b)
                    if b >= 1:
                        norm_evac("n1", l, b - 1)
                dve.wait_ge(gains_in, 96 * (l + 1))
                for ch, g0 in (("A", G_NQ), ("B", G_NK)):
                    for b in range(NB):
                        key = (ch, l, b)
                        rows_ = heads(qn(key)[:, 0:WIDTH])
                        head_sums(key, heads(sq[:, 0:WIDTH]))
                        qn_free(key)
                        if key == ("B", l, 2):
                            dve.wait_ge(k_out, 16 * (l + 1))
                        dve.wait_ge(rstd_ready.sem, rstd_ready.at(key))
                        per_head(key, rows_, heads(bank(key)[:, 0:WIDTH]), 0, HEADS).then_inc(prods.frees(key), 1)
                        dve.wait_ge(*prods.freed(key))
                        gain_mul(key, rows_, g0, DH)
                for b in range(NB + 1):
                    if b < NB:
                        key = ("D", l, b)
                        dve.wait_ge(*stats.filled(key))
                        v_.tensor_copy(pool_in[:, b, :], bank(key)[:, 0:POOL_W]).then_inc(pool_in_ready, 1)
                        qn_free(key)
                        dve.wait_ge(rstd_ready.sem, rstd_ready.at(key))
                        v_.tensor_scalar(qn(key)[:, 0:QR], bank(key)[:, POOL_W:POOL_W + QR], stat_cols(rst, key, 1),
                                         None, ALU.mult).then_inc(prods.frees(key), 1)
                    if b >= 1:
                        key = ("uq", l, b - 1)
                        head_sums(key, heads(sq))
                        q = heads(qn(key))
                        ps = sp_(key)[:, :, 0:288].rearrange("p a (h e) -> p a h e", h=3)
                        qn_free(key)
                        dve.wait_ge(rstd_ready.sem, rstd_ready.at(key))
                        for a in range(2):
                            ins = per_head(key, q[:, 3 * a:3 * a + 3, :], ps[:, a, :, :], 3 * a, 3)
                        ins.then_inc(pairs.frees(key), 1)
                        dve.wait_ge(*pairs.freed(key))
                        gain_mul(key, q, G_MQ, QK)
                dve.wait_ge(cached_in, 48 * (l + 1))
                for b in range(NKB + 1):
                    if b < NB:
                        key = ("E", l, b)
                        dve.wait_ge(*stats.filled(key))
                        v_.tensor_copy(krope[:, b * ROPE:(b + 1) * ROPE],
                                       bank(key)[:, KVR:KVR + ROPE]).then_inc(rope_keys, 1)
                        qn_free(key)
                        dve.wait_ge(rstd_ready.sem, rstd_ready.at(key))
                        v_.tensor_scalar(qn(key)[:, 0:KVR], bank(key)[:, 0:KVR], stat_cols(rst, key, 1),
                                         None, ALU.mult).then_inc(prods.frees(key), 1)
                        dve.wait_ge(*prods.freed(key))
                        gain_mul(key, qn(key)[:, 0:KVR], G_CKV, KVR)
                    if b >= 1:
                        key, before = ("ukv", l, b - 1), qns.before(("ukv", l, b - 1))
                        qn_free(key)
                        if before == ("E", l, 0):
                            dve.wait_ge(latent_out, 32 * (l + 1))
                        km = heads(qn(key))
                        ps = sp_(key)[:, :, 0:WIDTH].rearrange("p a (h e) -> p a h e", h=3)
                        dve.wait_ge(values_ready, l * NKB + b)
                        for a in range(2):
                            ins = v_.tensor_copy(km[:, 3 * a:3 * a + 3, 0:DH], ps[:, a, :, 0:DH])
                        ins.then_inc(pairs.frees(key), 1)
                        if b - 1 < NB:
                            dve.wait_ge(rope_keys, l * NB + b)
                        kr = krope[:, (b - 1) * ROPE:b * ROPE].unsqueeze(1).broadcast_to([P, HEADS, ROPE])
                        v_.tensor_copy(km[:, :, DH:], kr).then_inc(assembled, 1)
                        head_sums(key, heads(sq))
                        dve.wait_ge(assembled, l * NKB + b)
                        dve.wait_ge(rstd_ready.sem, rstd_ready.at(key))
                        per_head(key, km, km, 0, HEADS).then_inc(keys_scaled, 1)
                        dve.wait_ge(keys_scaled, l * NKB + b)
                        gain_mul(key, km, G_MK, QK)
                for g in range(2):
                    for b in range(NB):
                        use = ("py", l, g, b)
                        a0 = WIDTH + 2 * POOL_G * g
                        dve.wait_ge(*prods.filled(use))
                        v_.tensor_tensor(HO[:, b * D + a0:b * D + a0 + 2 * POOL_G], bank(use)[:, 0:2 * POOL_G],
                                         gains[:, G_POOL + 2 * POOL_G * g:G_POOL + 2 * POOL_G * (g + 1)],
                                         ALU.mult).then_inc(prods.frees(use), 1)
                with_bias = l * PAIRS_NA
                for i in range(ITEMS + 3):
                    if i < ITEMS:
                        kind, b, h = items[i]
                        blocks = key_blocks(kind, b)
                        n = len(blocks) * P
                        use = ("s", l, i)
                        dve.wait_ge(*pairs.filled(use))
                        s2 = sp_(use)[:, :, :].rearrange("p a n -> p (a n)")
                        if kind == "na" and b > 0:
                            if b == 1 and h == 0:
                                dve.wait_ge(bias_in, 16 * HEADS * ROWS * (l + 1))
                                dve.wait_ge(const_in, 32)
                            with_bias += 1
                            strips = near(b - 1)
                            first = strips[0] - (b - 1) + 1
                            m = len(strips)
                            loc = s2[:, 0:m * P].rearrange("p (m r j) -> p m r j", m=m, r=ROWS)
                            bv = bass.AP(tensor=GB, offset=h * ROWS * SPAN + SPAN - 1 - STRIP * first,
                                         ap=[[2304, P], [-STRIP, m], [SPAN, ROWS], [-1, STRIP]])
                            v_.tensor_tensor(loc, loc, bv, ALU.add).then_inc(bias_added, 1)
                            mo = (b - 1) * SPAN + STRIP * first
                            mv = masks[:, mo:mo + STRIP * m].rearrange("p (m j) -> p m j", m=m).unsqueeze(2)
                            dve.wait_ge(bias_added, with_bias)
                            v_.tensor_tensor(loc, loc, mv.broadcast_to([P, m, ROWS, STRIP]),
                                             ALU.add).then_inc(mask_added, 1)
                            dve.wait_ge(mask_added, with_bias)
                        if i >= 2:
                            dve.wait_ge(*pairs.freed(("s", l, i - 2)))
                        v_.tensor_reduce(nmax[:, i % 2:i % 2 + 1], s2[:, 0:n], AX.X, ALU.max,
                                         negate=True).then_inc(maxima, 1)
                    if 1 <= i <= ITEMS:
                        for part, (lo, hi) in enumerate(pt_parts(*items[i - 1][:2])):
                            if pt_engine(items[i - 1], part) == "vector":
                                use = ("pt", l, i - 1, part)
                                if i >= 3:
                                    dve.wait_ge(*head_done(l, i - 3))
                                dve.wait_ge(*flips.filled(use))
                                v_.tensor_copy(prob_T[(i - 1) % 2][:, lo:hi, :],
                                               tbank(use)[:, 0:(hi - lo) * P].rearrange("p (k q) -> p k q", q=P)
                                               ).then_inc(flips.frees(use), 1)
                    if i >= 3 and items[i - 3][2] == HEADS - 1:
                        kind, b, h = items[i - 3]
                        use, rkey = ("pv", l, kind, b), (l, kind, b)
                        rs = HEADS * rss.slot(rkey)
                        dve.wait_ge(*prods.filled(use))
                        v_.reciprocal(rinv[:, :], rsum[:, rs:rs + HEADS]).then_inc(inv_ready, 1)
                        dve.wait_ge(inv_ready, rss.no[rkey] + 1)
                        a0 = b * D + (0 if kind == "na" else WIDTH + POOL_W)
                        v_.tensor_tensor(heads(HO[:, a0:a0 + WIDTH]), heads(bank(use)[:, 0:WIDTH]),
                                         rinv[:, :].unsqueeze(2).broadcast_to([P, HEADS, DH]),
                                         ALU.mult).then_inc(prods.frees(use), 1)
                mod_cols(l, "n2")
                for b in range(NB + 1):
                    if b < NB:
                        for j in range(2):
                            use, step = ("o", l, b, j), ("mixer", l, b, j)
                            if b == 0:
                                dve.wait_ge(*prods.freed(("g", l, 0, j, 1)))
                            if j or b:
                                dve.wait_ge(x_updated.sem, x_updated.at(step) - 1)
                            dve.wait_ge(*prods.filled(use))
                            v_.tensor_tensor(gated, bank(use), gate_row[:, 0, min(b, 1), j * 512:(j + 1) * 512],
                                             ALU.mult).then_inc(prods.frees(use), 1)
                            xs = X[:, b * D + j * 512:b * D + (j + 1) * 512]
                            dve.wait_ge(*prods.freed(use))
                            v_.tensor_tensor(xs, xs, gated, ALU.add).then_inc(x_updated.sem, 1)
                        norm("n2", l, b)
                    if b >= 1:
                        norm_evac("n2", l, b - 1)

                u0 = l * UNITS
                if l == 0:
                    dve.sem_inc(u_used, URING)
                    dve.sem_inc(v_used, RING)
                dve.wait_ge(*prods.filled(("q", l, PH - 1, 0)))
                topk_unit(0, l, u0, 0, 0)
                stage(0, u0)
                topk_unit(1, l, u0 + 1, 0, 1)

                def peer_pair(it, b, last=False):
                    for e in range(2):
                        unit = it * 2 + (u0 + b * PH + e)
                        for k in range(TOPK):
                            dve.wait_ge(u_in[k % URING], unit * (16 * TOPK // URING) + 16 * (k // URING + 1))
                            row, col = u_ring[k % URING], e * TOPK + k
                            v_.tensor_tensor_reduce(out=row, in0=row, in1=tokens, scale=1.0, scalar=0.0,
                                                    op0=ALU.mult, op1=ALU.add,
                                                    accum_out=dots[:, col:col + 1]).then_inc(u_used, 1)
                            if k == 5 and not (last and e == 1):
                                dve.wait_ge(v_used, unit * TOPK + RING)
                                stage(1 - e, unit + 1)
                        mine = slice(e * TOPK, (e + 1) * TOPK)
                        dve.wait_ge(gates_staged, unit + 1)
                        dve.wait_ge(gelu_ready, unit + 1)
                        v_.tensor_tensor(wgt[:, mine], gel[:, mine], gate_st[:, mine],
                                         ALU.mult).then_inc(weights_ready, 1)
                        if not last:
                            topk_unit(e, l, unit + 2, it, (it * 2 + (e + 2)) % PH)

                def finish(b):
                    if b == 0:
                        dve.wait_ge(*prods.freed(("g", l, 1, 1, 1)))
                    dve.wait_ge(sum_copied, l * NB + b + 1)
                    v_.tensor_tensor(block_sum, block_sum, gate_row[:, 1, min(b, 1), :], ALU.mult).then_inc(sum_gated, 1)
                    dve.wait_ge(sum_gated, l * NB + b + 1)
                    v_.tensor_tensor(xb(b), xb(b), block_sum, ALU.add).then_inc(x_updated.sem, 1)
                    dve.wait_ge(x_updated.sem, x_updated.at(("peer", l, b)))

                for b in range(NB):
                    dve.wait_ge(*prods.freed(("t", l, b, 1)))
                    if b + 1 < NB:
                        with dve.Fori(0, PH // 2) as it:
                            peer_pair(it, b)
                    else:
                        with dve.Fori(0, PH // 2 - 1) as it:
                            peer_pair(it, b)
                        peer_pair(PH // 2 - 1, b, last=True)
                    if b:
                        finish(b - 1)
                finish(NB - 1)

        @block.tensor
        def _(pe):
            t_ = nc.tensor

            def prod_bank(use):
                if prods.before(use):
                    pe.wait_ge(*prods.freed(prods.before(use)))
                return bank(use)

            def flip_bank(use):
                if flips.before(use):
                    pe.wait_ge(*flips.freed(flips.before(use)))
                return tbank(use)

            def pair_banks(use):
                if pairs.before(use):
                    pe.wait_ge(*pairs.freed(pairs.before(use)))
                return sp_(use)

            def transposes(use, views):
                dst = flip_bank(use)
                for j, v in enumerate(views):
                    n = v.shape[1]
                    ins = t_.transpose(dst[0:n, j * P:(j + 1) * P], v, ident[:, :])
                ins.then_inc(flips.fills(use), 1)

            def block_T(k, l, b):
                x_ = xn[xns.slot((k, l, b))]
                pe.wait_ge(tokens_scaled.sem, tokens_scaled.at((k, l, b)))
                for hf in range(2):
                    transposes((k, l, b, hf), [x_[:, (4 * hf + j) * P:(4 * hf + j + 1) * P] for j in range(4)])

            def heads_T(name, key):
                k, l, b = key
                if 1 <= b < NB:
                    pe.wait_ge(roped.sem, roped.at(key))
                else:
                    pe.wait_ge(gained.sem, gained.at(key))
                rows_ = qn(key).rearrange("p (h e) -> p h e", h=HEADS)
                for part, (h0, h1) in enumerate(((0, 4), (4, 6))):
                    transposes((name, l, b, part), [rows_[:, h, :] for h in range(h0, h1)])

            def mod_row(l, m):
                q, use = CH[(l, f"m{m}")], ("r", l, m)
                w, dst = wr(q), prod_bank(use)
                pe.wait_ge(*chunk_in(q))
                for kk in range(KC):
                    ins = t_.matmul(dst[0:2, :], sct[:, :].rearrange("p (c k) -> p k c", c=2)[:, kk, :], w[:, kk, :],
                                    start=kk == 0, stop=kk == KC - 1)
                ins.then_inc(prods.fills(use), 1)

            def mod_columns(l, k, m):
                use, j = ("mc", l, k), m - (0 if k == "n1" else 6)
                dst = flip_bank(use) if j == 0 else tbank(use)
                pe.wait_ge(*prods.freed(("r", l, m)))
                for g in range(4):
                    col = (4 * j + g) * 2
                    ins = t_.transpose(dst[:, col:col + 2], mod_rows[:, m % 2, g * P:(g + 1) * P], ident[0:2, 0:2])
                if j == 3:
                    ins.then_inc(flips.fills(use), 1)

            def gate_on_all(l, j, cnd):
                use, m = ("g", l, 0, j, cnd), 4 + j
                dst = prod_bank(use)
                pe.wait_ge(*prods.freed(("r", l, m)))
                t_.matmul(dst, ident[0:2, cnd:cnd + 1].broadcast_to([2, P]), mod_rows[:, m % 2, :],
                          start=True, stop=False)
                for g in range(4):
                    row = V_BMOD + 2 * KC + 4 * j + g
                    ins = t_.matmul(dst[:, g * P:(g + 1) * P], ident[:, row:row + 1].broadcast_to([P, P]),
                                    rows[:, :], start=False, stop=g == 3)
                ins.then_inc(prods.fills(use), 1)

            def gate_rows(l, j, cnd, name):
                q, use = CH[(l, name)], ("g", l, 1, j, cnd)
                w, dst = wr(q), prod_bank(use)
                pe.wait_ge(*chunk_in(q))
                for kk in range(KC):
                    ins = t_.matmul(dst, sct[:, cnd * KC + kk:cnd * KC + kk + 1].broadcast_to([P, P]), w[:, kk, :],
                                    start=kk == 0, stop=kk == KC - 1)
                    if kk == 0:
                        for g in range(4):
                            row = V_BMOD + 5 * KC + 4 * j + g
                            t_.matmul(dst[:, g * P:(g + 1) * P], ident[:, row:row + 1].broadcast_to([P, P]),
                                      rows[:, :], start=False, stop=False)
                ins.then_inc(prods.fills(use), 1)

            def project(name, l, b, n):
                use, q = (name, l, b), CH[(l, name)]
                w, dst = wr(q), prod_bank(use)
                if b == 0:
                    pe.wait_ge(*chunk_in(q))
                if name == "A":
                    pe.wait_ge(*flips.freed(("n1", l, b, 0)))
                    pe.wait_ge(*flips.freed(("n1", l, b, 1)))
                for kk in range(KC):
                    ins = t_.matmul(dst[:, 0:n], hT(b, kk), w[:, kk, 0:n], start=kk == 0, stop=kk == KC - 1)
                ins.then_inc(prods.fills(use), 1)

            for l in range(LAYERS):
                if l == 0:
                    pe.wait_ge(setup, IDENTITY)
                pe.wait_ge(vectors_in, 96 * (l + 1))
                transposes(("vec", l), [rows[:, :]])
                pe.wait_ge(subkeys_in, 16 * (l + 1))
                transposes(("subk", l), [sk_raw[:, :]])
                if l == 0:
                    pe.wait_ge(silu_done, 1)
                for m in range(5):
                    if m < 4:
                        mod_row(l, m)
                    if m >= 1:
                        mod_columns(l, "n1", m - 1)
                for b in range(NB):
                    block_T("n1", l, b)
                for ch in "AB":
                    for b in range(NB + 1):
                        if b < NB:
                            project(ch, l, b, WIDTH)
                        if b >= 1:
                            key = (ch, l, b - 1)
                            pe.wait_ge(gained.sem, gained.at(key))
                            transposes((ch + "t", l, b - 1), [qn(key)[:, j * P:(j + 1) * P] for j in range(3)])
                pe.wait_ge(cached_in, 48 * (l + 1))
                transposes(("ct", l), [ckc[:, j * P:(j + 1) * P] for j in range(3)])
                for b in range(NB):
                    project("C", l, b, WIDTH)
                pe.wait_ge(small_in, 64 * (l + 1))
                for b in range(NB + 2):
                    if b < NB:
                        project("D", l, b, POOL_W + QR)
                    if 1 <= b <= NB:
                        key = ("D", l, b - 1)
                        pe.wait_ge(*rows_scaled(key))
                        transposes(("cqt", l, b - 1), [qn(key)[:, j * P:(j + 1) * P] for j in range(2)])
                        use = ("uq", l, b - 1)
                        dst = pair_banks(use)
                        pe.wait_ge(*flips.freed(("cqt", l, b - 1)))
                        for a in range(2):
                            for kk in range(2):
                                ins = t_.matmul(dst[:, a, 0:288], lat_T[:, kk, :], w_uq[:, kk, 288 * a:288 * (a + 1)],
                                                start=kk == 0, stop=kk == 1)
                        ins.then_inc(pairs.fills(use), 1)
                    if b >= 2:
                        heads_T("qmt", ("uq", l, b - 2))
                for b in range(NKB + 2):
                    if b < NB:
                        project("E", l, b, KVR + ROPE)
                    if 1 <= b <= NKB:
                        key = ("E", l, b - 1)
                        if b - 1 < NB:
                            pe.wait_ge(gained.sem, gained.at(key))
                            transposes(("ckt", l, b - 1), [qn(key)[:, 0:KVR]])
                        else:
                            transposes(("ckt", l, b - 1), [ckvc[:, :]])
                        use = ("ukv", l, b - 1)
                        dst = pair_banks(use)
                        pe.wait_ge(*flips.freed(("ckt", l, b - 1)))
                        for a in range(2):
                            ins = t_.matmul(dst[:, a, 0:WIDTH], lat_T[:, 0, :], w_ukv[:, WIDTH * a:WIDTH * (a + 1)],
                                            start=True, stop=True)
                        ins.then_inc(pairs.fills(use), 1)
                    if b >= 2:
                        heads_T("kmt", ("ukv", l, b - 2))
                pe.wait_ge(pool_in_ready, NB * (l + 1))
                pe.wait_ge(const_in, 32)
                for g in range(2):
                    q = CH[(l, f"P{g}")]
                    w = wr(q)
                    use = ("pdp", l, g)
                    dst = pair_banks(use)
                    for i in range(2):
                        wg = 2 * g + i
                        ins = t_.matmul(dst[0:POOL_G, 0, i * P:(i + 1) * P],
                                        pool_in[:, 0, wg * POOL_G:(wg + 1) * POOL_G], mpp[:, wg * P:(wg + 1) * P],
                                        start=True, stop=True)
                    ins.then_inc(pairs.fills(use), 1)
                    use = ("pds", l, g)
                    dst = pair_banks(use)
                    pe.wait_ge(*chunk_in(q))
                    for i in range(2):
                        wg = 2 * g + i
                        for m in range(4):
                            ins = t_.matmul(dst[0:POOL_G, i, :], pool_in[:, 1 + m, wg * POOL_G:(wg + 1) * POOL_G],
                                            w[:, 4 * i + m, :], start=m == 0, stop=m == 3)
                    ins.then_inc(pairs.fills(use), 1)
                    pe.wait_ge(*pairs.freed(("pdp", l, g)))
                    pe.wait_ge(*pairs.freed(("pds", l, g)))
                    for b in range(NB):
                        use = ("py", l, g, b)
                        dst = prod_bank(use)
                        for i in range(2):
                            wg = 2 * g + i
                            ins = t_.matmul(dst[:, i * POOL_G:(i + 1) * POOL_G], d_T[:, i, b * P:(b + 1) * P],
                                            poolw[0:POOL_G, wg * POOL_G:(wg + 1) * POOL_G], start=True, stop=True)
                        ins.then_inc(prods.fills(use), 1)
                pe.wait_ge(*flips.freed(("kmt", l, CTX, 0)))
                pe.wait_ge(*flips.freed(("kmt", l, CTX, 1)))
                pe.wait_ge(values_ready, NKB * (l + 1))
                for i in range(ITEMS + 2):
                    if i < ITEMS:
                        kind, b, h = items[i]
                        blocks = key_blocks(kind, b)
                        use = ("s", l, i)
                        dst = pair_banks(use)
                        if kind == "mla":
                            lhs, keys = qm_T[:, h, b * P:(b + 1) * P], km_T[:, h, :]
                        else:
                            lo = DH * (h % 2)
                            lhs = qn_T[lo:lo + DH, h // 2, b * P:(b + 1) * P]
                            keys = kn_T[lo:lo + DH, h // 2, :]
                        if b == 0:
                            spans = [(0, 0, 0, P)]
                        elif kind == "mla":
                            spans = [(0, 0, P, 4 * P), (1, 0, CTX * P, P)]
                        else:
                            m = len(blocks) - 1
                            spans = [(0, 0, blocks[0] * P, m * P), (0, m * P, CTX * P, P)]
                        for a, col, key0, n in spans:
                            ins = t_.matmul(dst[:, a, col:col + n], lhs, keys[:, key0:key0 + n], start=True, stop=True)
                        ins.then_inc(pairs.fills(use), 1)
                    if 1 <= i <= ITEMS:
                        pe.wait_ge(*pairs.freed(("s", l, i - 1)))
                        for part, (lo, hi) in enumerate(pt_parts(*items[i - 1][:2])):
                            transposes(("pt", l, i - 1, part),
                                       [prob[(i - 1) % 2][:, k * P:(k + 1) * P] for k in range(lo, hi)])
                    if i >= 2:
                        kind, b, h = items[i - 2]
                        use = ("pv", l, kind, b)
                        dst = prod_bank(use) if h == 0 else bank(use)
                        blocks = key_blocks(kind, b)
                        for part in range(len(pt_parts(kind, b))):
                            pe.wait_ge(*flips.freed(("pt", l, i - 2, part)))
                        if kind == "na" and b == 0 and h == 0:
                            pe.wait_ge(cached_v_in, 16 * (l + 1))
                        for k, kb in enumerate(blocks):
                            val = v_mla[:, kb, h, :] if kind == "mla" else v_na[:, kb, h * DH:(h + 1) * DH]
                            ins = t_.matmul(dst[:, h * DH:(h + 1) * DH], prob_T[(i - 2) % 2][:, k, :], val,
                                            start=k == 0, stop=k == len(blocks) - 1)
                        ins.then_inc(prods.fills(use) if h == HEADS - 1 else head_attended, 1)
                mod_row(l, 4)
                mod_row(l, 5)
                for j in range(2):
                    for cnd in range(2):
                        gate_on_all(l, j, cnd)
                    mod_row(l, 6 + j)
                for m in range(6, 10):
                    if m >= 8:
                        mod_row(l, m)
                        mod_columns(l, "n2", m - 1)
                    elif m == 6:
                        mod_columns(l, "n2", m)
                mod_columns(l, "n2", 9)
                q0, q1 = CH[(l, "o0")], CH[(l, "o1")]
                pe.wait_ge(*prods.freed(("pv", l, "na", NB - 1)))
                for b in range(-1, NB + 1):
                    if b + 1 < NB:
                        for hf in range(2):
                            transposes(("ot", l, b + 1, hf), [mixed(b + 1, 4 * hf + j) for j in range(4)])
                    if 0 <= b < NB:
                        pe.wait_ge(*flips.freed(("ot", l, b, 0)))
                        pe.wait_ge(*flips.freed(("ot", l, b, 1)))
                        for j, q in enumerate((q0, q1)):
                            use, w = ("o", l, b, j), wr(q)
                            dst = prod_bank(use)
                            if b == 0:
                                pe.wait_ge(*chunk_in(q))
                            for kk in range(KC):
                                ins = t_.matmul(dst, o_T[ots.slot((l, b))][:, kk, :], w[:, kk, :], start=kk == 0,
                                                stop=kk == KC - 1)
                            ins.then_inc(prods.fills(use), 1)
                    if b >= 1:
                        block_T("n2", l, b - 1)
                pe.wait_ge(*flips.freed(("n2", l, NB - 1, 0)))
                pe.wait_ge(*flips.freed(("n2", l, NB - 1, 1)))
                h_blocks = HO[:, :].rearrange("p (b k t) -> p b k t", b=NB, k=KC)

                def queries(h, part):
                    q, use = CH[(l, f"q{h // 4}")], ("q", l, h, part)
                    b0, b1 = (0, 1) if part == 0 else (1, NB)
                    w, dst = wr(q), prod_bank(use)
                    pe.wait_ge(*chunk_in(q))
                    for kk in range(KC):
                        ins = t_.matmul(dst[:, 0:(b1 - b0) * P], w[:, kk, (h % 4) * P:(h % 4 + 1) * P],
                                        h_blocks[:, b0:b1, kk, :], start=kk == 0, stop=kk == KC - 1)
                    ins.then_inc(prods.fills(use), 1)

                for h in range(PH):
                    queries(h, 0)
                def peer_scores(b):
                    pe.wait_ge(*prods.freed(("q", l, PH - 1, min(b, 1))))
                    for h in range(PH):
                        ins = t_.matmul(key_scores[:, h * 2 * NKEYS:(h + 1) * 2 * NKEYS],
                                        pq_T[:, h, b * P:(b + 1) * P], skT[:, :], start=True, stop=True)
                    ins.then_inc(score_full, PH)

                def peer_tokens(b):
                    for hf in range(2):
                        use = ("t", l, b, hf)
                        dst = prod_bank(use)
                        for k in range(4):
                            ins = t_.transpose(dst[:, k * P:(k + 1) * P], hT(b, 4 * hf + k), ident[:, :])
                        ins.then_inc(prods.fills(use), 1)

                def v_rows(unit, e, last=False):
                    for k in range(TOPK):
                        pe.wait_ge(diag_ready, unit * TOPK + (k + 1))
                        pe.wait_ge(v_in[k % RING], unit * (16 * TOPK // RING) + 16 * (k // RING + 1))
                        for hf in range(2):
                            ins = t_.matmul(acc[:, hf * 512:(hf + 1) * 512], diags[:, k * P:(k + 1) * P],
                                            v_ring[:, k % RING, hf * 512:(hf + 1) * 512], start=False,
                                            stop=last and k == TOPK - 1)
                        ins.then_inc(v_used, 1)

                peer_scores(0)
                peer_tokens(0)
                for cnd in range(2):
                    gate_rows(l, 0, cnd, "m10")
                for b in range(NB):
                    u0 = l * UNITS + b * PH
                    if l or b:
                        pe.wait_ge(sum_copied, l * NB + b)
                    if b == 0:
                        pe.wait_ge(*prods.freed(("g", l, 1, 0, 0)))
                    for hf in range(2):
                        t_.matmul(acc[:, hf * 512:(hf + 1) * 512], skT[0:P // 2, NKEYS:2 * NKEYS],
                                  gate_row[0:P // 2, 1, 0, 0:512], start=True, stop=False)
                    if b == 0:
                        for unit in range(PH - 2):
                            v_rows(u0 + unit, unit % 2)
                            for use in BESIDE.get(unit, []):
                                if use[0] == "q":
                                    queries(*use[1:])
                                else:
                                    gate_rows(l, *use[2:], "m11")
                    else:
                        with pe.Fori(0, PH // 2 - 1) as it:
                            for e in range(2):
                                v_rows(it * 2 + (u0 + e), e)
                    if b + 1 < NB:
                        pe.wait_ge(score_free, u0 + PH)
                        peer_scores(b + 1)
                        peer_tokens(b + 1)
                    v_rows(u0 + PH - 2, 0)
                    v_rows(u0 + PH - 1, 1, last=True)


def _tables():
    def pooling(n):
        t = np.arange(n)
        out = np.zeros((len(POOLS), n, n), np.float32)
        for i, w in enumerate(POOLS):
            lo, hi = np.clip(t - w // 2, 0, n), np.clip(t + (w - w // 2), 0, n)
            inside = (t[:, None] >= lo[None]) & (t[:, None] < hi[None])
            out[i] = inside / (hi - lo)[None].astype(np.float32) - np.eye(n)
        return out
    n = ROWS * GRID_W
    at = (np.arange(ROWS)[None, :, None] * GRID_W + np.arange(4)[:, None, None] * STRIP
          + np.arange(STRIP)[None, None, :]).reshape(-1)
    sample = pooling(n)[:, at][:, :, at]
    sample = sample.reshape(4, 4, P, n).transpose(2, 0, 1, 3).reshape(P, 16, n)
    prompt = pooling(P).transpose(1, 0, 2).reshape(P, 4 * P)
    inv = (10000.0 ** (-np.arange(0, ROPE // 2, 2, dtype=np.float32) / (ROPE // 2))).astype(np.float32)
    ang = [pos.astype(np.float32)[:, None] * inv for pos in (at // GRID_W, at % GRID_W)]
    cos = np.concatenate([np.cos(a) for a in ang for _ in range(2)], 1)
    sin = np.concatenate([s * np.sin(a) for a in ang for s in (-1, 1)], 1)
    rope = np.concatenate([cos, sin], 1).astype(np.float32).reshape(4, P, 2 * ROPE)
    mask = np.zeros((P, 4, SPAN), np.float32)
    for s in range(4):
        q = s * STRIP + np.arange(P) % STRIP
        start = np.clip(q - WIN_C // 2, 0, GRID_W - WIN_C)
        key = (s - 1) * STRIP + np.arange(SPAN)
        ok = (key[None] >= start[:, None]) & (key[None] < start[:, None] + WIN_C)
        mask[:, s] = np.where(ok, 0.0, NEG)
    return (np.ascontiguousarray(sample, np.float32), np.ascontiguousarray(prompt, np.float32), rope,
            mask.reshape(P, 4 * SPAN))


def kernel(**inputs):
    import concourse.bacc as _bacc
    from concourse.bass_utils import run_bass_kernel_spmd as _run

    a = {k: np.asarray(v) for k, v in inputs.items()}
    L = LAYERS
    t_pool, t_pool_prompt, t_rope, t_mask = _tables()

    def strips(x):
        return x.reshape(ROWS, 4, STRIP, D).transpose(1, 0, 2, 3).reshape(4 * P, D)

    rb = a["na_rel_bias"][:, :, ::-1, ::-1].reshape(-1)
    arrays = {
        "x_prompt": a["x_prompt"].reshape(P, D), "x_sample": strips(a["x_sample"]), "c": a["c"].reshape(D),
        "c_ctx": a["c_ctx"].reshape(D), "cache_nat_k": a["cache_nat_k"].reshape(L, P, WIDTH),
        "cache_nat_v": a["cache_nat_v"].reshape(L, P, WIDTH),
        "cache_mla_ckv": a["cache_mla_ckv"].reshape(L, P, KVR),
        "cache_mla_krope": a["cache_mla_krope"].reshape(L, P, ROPE), "w_mod": a["w_mod"], "b_mod": a["b_mod"],
        "norm1": a["norm1"], "norm2": a["norm2"], "w_in": a["w_in"], "na_q_norm": a["na_q_norm"],
        "na_k_norm": a["na_k_norm"],
        "rel_bias": np.concatenate([np.zeros(RB_PAD, rb.dtype), rb, np.zeros(RB_PAD, rb.dtype)]),
        "pool_w": a["pool_w"], "pool_scale": a["pool_scale"], "mla_cq_norm": a["mla_cq_norm"],
        "mla_ckv_norm": a["mla_ckv_norm"], "mla_w_uq": a["mla_w_uq"].reshape(L, QR, HEADS * QK),
        "mla_w_ukv": a["mla_w_ukv"].reshape(L, KVR, HEADS * 2 * DH), "mla_q_norm": a["mla_q_norm"],
        "mla_k_norm": a["mla_k_norm"], "w_out": a["w_out"], "peer_wq": a["peer_wq"],
        "peer_subkeys": a["peer_subkeys"], "peer_u": a["peer_u"].reshape(L * NEXP, D),
        "peer_v": a["peer_v"].reshape(L * NEXP, D), "t_pool": t_pool, "t_pool_prompt": t_pool_prompt,
        "t_rope": t_rope, "t_mask": t_mask,
    }
    outs = {"y_prompt": (P, D), "y_sample": (4 * P, D), "new_k": (L, P, WIDTH), "new_v": (L, P, WIDTH),
            "new_ckv": (L, P, KVR), "new_krope": (L, P, ROPE)}
    nc = _bacc.Bacc("TRN2", target_bir_lowering=False, num_devices=1)
    args, in_map = {}, {}
    for name, x in arrays.items():
        x = np.ascontiguousarray(x)
        in_map[f"in_{name}"] = x
        args[name] = nc.dram_tensor(f"in_{name}", x.shape, mybir.dt.from_np(x.dtype), kind="ExternalInput").ap()
    for name, shape in outs.items():
        args[name] = nc.dram_tensor(f"out_{name}", shape, mybir.dt.float32, kind="ExternalOutput").ap()
    build(nc, **args)
    r = _run(nc, [in_map], core_ids=[0]).results[0]
    y = r["out_y_sample"].reshape(4, ROWS, STRIP, D).transpose(1, 0, 2, 3).reshape(1, ROWS * GRID_W, D)
    return (r["out_y_prompt"].reshape(1, P, D), y, r["out_new_k"].reshape(1, L, P, HEADS, DH),
            r["out_new_v"].reshape(1, L, P, HEADS, DH), r["out_new_ckv"].reshape(1, L, P, KVR),
            r["out_new_krope"].reshape(1, L, P, ROPE))
```
